# Optimizing a Trainium2 kernel written in Bass

```python
import jax, jax.numpy as jnp
from jax import lax
import numpy as np

D_MODEL = 1024
BATCH = 1
SEQ = 256
DEPTH = 2

CONV_WIDTH = D_MODEL // 2
CONV_GROUPS = 8
CONV_KERNEL = 31
N_HEADS = 8
HEAD_DIM = 64
N_KV_HEADS = 2
GQA = N_HEADS // N_KV_HEADS
ATTN_WIDTH = N_HEADS * HEAD_DIM
KV_WIDTH = N_KV_HEADS * HEAD_DIM
MIX_WIDTH = CONV_WIDTH + ATTN_WIDTH
N_BRANCH = 3
IN_WIDTH = 2 * CONV_WIDTH + ATTN_WIDTH + 6 * KV_WIDTH + N_HEADS * N_BRANCH
CMP_BLOCK = 32
CMP_STRIDE = 16
CMP_HIDDEN = 256
SEL_BLOCK = 64
SEL_TOPK = 8
WINDOW = 512
Q_BLOCK = 128
FORCE_BONUS = 1e4
NEG_INF = -1e30
D_FF = 2816
N_EXPERTS = 8
TOP_K = 2
D_FF_EXPERT = 3584
N_DENSE = (DEPTH + 1) // 2
N_MOE = DEPTH // 2
EPS = 1e-6

kernel_name = "hymba_conformer_nsa_moe_block"

def rms_norm(x, g):
    xf = x.astype(jnp.float32)
    xf = xf * lax.rsqrt(jnp.mean(xf * xf, axis=-1, keepdims=True) + EPS)
    return (xf * g.astype(jnp.float32)).astype(x.dtype)

def masked_softmax(s, mask):
    s = jnp.where(mask, s.astype(jnp.float32), NEG_INF)
    m = jnp.max(s, axis=-1, keepdims=True)
    p = jnp.where(mask, jnp.exp(s - m), 0.0)
    return p / jnp.maximum(jnp.sum(p, axis=-1, keepdims=True), 1e-30)

def conv_module(val, gate, dw_w, dw_b, ln_g, ln_b):
    B, S, C = val.shape
    u = val * jax.nn.sigmoid(gate)
    u = jnp.pad(u, ((0, 0), (CONV_KERNEL - 1, 0), (0, 0)))
    y = lax.conv_general_dilated(u, dw_w[:, None, :], window_strides=(1,), padding="VALID",
                                 dimension_numbers=("NWC", "WIO", "NWC"),
                                 feature_group_count=C) + dw_b
    yg = y.reshape(B, S, CONV_GROUPS, C // CONV_GROUPS).astype(jnp.float32)
    mu = jnp.mean(yg, axis=-1, keepdims=True)
    var = jnp.mean(jnp.square(yg - mu), axis=-1, keepdims=True)
    yn = ((yg - mu) * lax.rsqrt(var + EPS)).reshape(B, S, C)
    yn = yn * ln_g.astype(jnp.float32) + ln_b.astype(jnp.float32)
    return jax.nn.silu(yn).astype(val.dtype)

def nsa_attention(q, k_cmp, v_cmp, k_sel, v_sel, k_win, v_win, gate_logits, q_g, k_g,
                  pos_k, pos_v, ck_w1, ck_b1, ck_w2, ck_b2, cv_w1, cv_b1, cv_w2, cv_b2):
    dtype = q.dtype
    B, S = q.shape[:2]
    t = jnp.arange(S)

    def heads_kv(a):
        return a.reshape(B, S, N_KV_HEADS, HEAD_DIM).transpose(0, 2, 1, 3)

    qh = rms_norm(q.reshape(B, S, N_KV_HEADS, GQA, HEAD_DIM), q_g).transpose(0, 2, 3, 1, 4)
    qh = qh * (HEAD_DIM ** -0.5)
    ks = rms_norm(heads_kv(k_sel), k_g[1])
    vs = heads_kv(v_sel)
    kw = rms_norm(heads_kv(k_win), k_g[2])
    vw = heads_kv(v_win)

    n_cmp = (S - CMP_BLOCK) // CMP_STRIDE + 1
    c_start = jnp.arange(n_cmp) * CMP_STRIDE
    cidx = c_start[:, None] + jnp.arange(CMP_BLOCK)[None, :]

    def compress(a, pos, w1, b1, w2, b2):
        blk = heads_kv(a)[:, :, cidx] + pos
        blk = blk.reshape(B, N_KV_HEADS, n_cmp, CMP_BLOCK * HEAD_DIM)
        return jax.nn.silu(blk @ w1 + b1) @ w2 + b2

    kc = rms_norm(compress(k_cmp, pos_k, ck_w1, ck_b1, ck_w2, ck_b2), k_g[0])
    vc = compress(v_cmp, pos_v, cv_w1, cv_b1, cv_w2, cv_b2)
    s_c = jnp.einsum("bkgsd,bkcd->bkgsc", qh, kc)
    mask_c = (c_start + CMP_BLOCK - 1)[None, :] <= t[:, None]
    p_c = masked_softmax(s_c, mask_c)
    o_cmp = jnp.einsum("bkgsc,bkcd->bkgsd", p_c.astype(vc.dtype), vc)

    n_sel = S // SEL_BLOCK
    j = jnp.arange(n_sel)
    overlap = ((c_start[:, None] < (j[None, :] + 1) * SEL_BLOCK)
               & (c_start[:, None] + CMP_BLOCK > j[None, :] * SEL_BLOCK)).astype(jnp.float32)
    imp = jnp.einsum("bkgsc,cj->bksj", p_c, overlap)
    cur = (t // SEL_BLOCK)[:, None]
    forced = (j[None, :] == 0) | (j[None, :] == cur) | (j[None, :] == cur - 1)
    causal_blk = j[None, :] * SEL_BLOCK <= t[:, None]
    score = jnp.where(causal_blk, imp + jnp.where(forced, FORCE_BONUS, 0.0), NEG_INF)
    k_eff = min(SEL_TOPK, n_sel)
    _, sel_idx = lax.top_k(score, k_eff)

    n_qb = S // Q_BLOCK
    kblk = ks.reshape(B, N_KV_HEADS, n_sel, SEL_BLOCK, HEAD_DIM)
    vblk = vs.reshape(B, N_KV_HEADS, n_sel, SEL_BLOCK, HEAD_DIM)
    pad = ((0, 0), (0, 0), (WINDOW, 0), (0, 0))
    kw_pad = jnp.pad(kw, pad)
    vw_pad = jnp.pad(vw, pad)
    q_chunks = qh.reshape(B, N_KV_HEADS, GQA, n_qb, Q_BLOCK, HEAD_DIM).transpose(3, 0, 1, 2, 4, 5)
    idx_chunks = sel_idx.reshape(B, N_KV_HEADS, n_qb, Q_BLOCK, k_eff).transpose(2, 0, 1, 3, 4)
    bi = jnp.arange(B)[:, None, None, None]
    hi = jnp.arange(N_KV_HEADS)[None, :, None, None]
    band = jnp.arange(WINDOW + Q_BLOCK)

    def block_step(args):
        qc, ic, n = args
        start = n * Q_BLOCK
        tq = start + jnp.arange(Q_BLOCK)
        kg = kblk[bi, hi, ic]
        vg = vblk[bi, hi, ic]
        kpos = ic[..., None] * SEL_BLOCK + jnp.arange(SEL_BLOCK)
        m_s = (kpos <= tq[:, None, None]).reshape(B, N_KV_HEADS, 1, Q_BLOCK, k_eff * SEL_BLOCK)
        s_s = jnp.einsum("bkgqd,bkqnld->bkgqnl", qc, kg).reshape(
            B, N_KV_HEADS, GQA, Q_BLOCK, k_eff * SEL_BLOCK)
        p_s = masked_softmax(s_s, m_s).reshape(B, N_KV_HEADS, GQA, Q_BLOCK, k_eff, SEL_BLOCK)
        o_s = jnp.einsum("bkgqnl,bkqnld->bkgqd", p_s.astype(vg.dtype), vg)
        kb = lax.dynamic_slice_in_dim(kw_pad, start, WINDOW + Q_BLOCK, axis=2)
        vb = lax.dynamic_slice_in_dim(vw_pad, start, WINDOW + Q_BLOCK, axis=2)
        wpos = start - WINDOW + band
        m_w = ((wpos[None, :] <= tq[:, None]) & (wpos[None, :] > tq[:, None] - WINDOW)
               & (wpos[None, :] >= 0))
        s_w = jnp.einsum("bkgqd,bkjd->bkgqj", qc, kb)
        p_w = masked_softmax(s_w, m_w)
        o_w = jnp.einsum("bkgqj,bkjd->bkgqd", p_w.astype(vb.dtype), vb)
        return o_s, o_w

    o_sel, o_win = lax.map(block_step, (q_chunks, idx_chunks, jnp.arange(n_qb)))

    def unchunk(o):
        return o.transpose(1, 2, 3, 0, 4, 5).reshape(B, N_KV_HEADS, GQA, S, HEAD_DIM)

    g = jax.nn.sigmoid(gate_logits.astype(jnp.float32)).reshape(
        B, S, N_KV_HEADS, GQA, N_BRANCH).transpose(0, 2, 3, 1, 4)
    o = (g[..., 0:1] * o_cmp.astype(jnp.float32) + g[..., 1:2] * unchunk(o_sel).astype(jnp.float32)
         + g[..., 2:3] * unchunk(o_win).astype(jnp.float32))
    return o.transpose(0, 3, 1, 2, 4).reshape(B, S, ATTN_WIDTH).astype(dtype)

def swiglu(h, w1, w3, w2):
    return (jax.nn.silu(h @ w1) * (h @ w3)) @ w2

def moe_swiglu(h, router, w1, w3, w2):
    logits = (h @ router).astype(jnp.float32)
    top_vals, top_idx = lax.top_k(logits, TOP_K)
    top_w = jax.nn.softmax(top_vals, axis=-1)
    combine = jnp.sum(jax.nn.one_hot(top_idx, N_EXPERTS, dtype=jnp.float32) * top_w[..., None], axis=-2)
    y = jnp.zeros(h.shape, jnp.float32)
    for e in range(N_EXPERTS):
        y = y + combine[..., e:e + 1] * swiglu(h, w1[e], w3[e], w2[e]).astype(jnp.float32)
    return y.astype(h.dtype)

def setup_inputs(seed: int = 0) -> dict:
    key = jax.random.key(seed)
    ks = jax.random.split(key, 32)

    def nrm(k, shape, scale):
        return jax.random.normal(k, shape, jnp.float32) * scale

    L, Dh = DEPTH, HEAD_DIM
    return {
        "x": nrm(ks[0], (BATCH, SEQ, D_MODEL), 1.0),
        "attn_norm_g": 1.0 + nrm(ks[1], (L, D_MODEL), 0.02),
        "w_in": nrm(ks[2], (L, D_MODEL, IN_WIDTH), D_MODEL ** -0.5),
        "conv_dw_w": nrm(ks[3], (L, CONV_KERNEL, CONV_WIDTH), CONV_KERNEL ** -0.5),
        "conv_dw_b": nrm(ks[4], (L, CONV_WIDTH), 0.02),
        "conv_ln_g": 1.0 + nrm(ks[5], (L, CONV_WIDTH), 0.02),
        "conv_ln_b": nrm(ks[6], (L, CONV_WIDTH), 0.02),
        "q_norm_g": 1.0 + nrm(ks[7], (L, Dh), 0.02),
        "k_norm_g": 1.0 + nrm(ks[8], (L, N_BRANCH, Dh), 0.02),
        "cmp_pos_k": nrm(ks[9], (L, CMP_BLOCK, Dh), 0.1),
        "cmp_pos_v": nrm(ks[10], (L, CMP_BLOCK, Dh), 0.1),
        "cmp_k_w1": nrm(ks[11], (L, CMP_BLOCK * Dh, CMP_HIDDEN), (CMP_BLOCK * Dh) ** -0.5),
        "cmp_k_b1": nrm(ks[12], (L, CMP_HIDDEN), 0.02),
        "cmp_k_w2": nrm(ks[13], (L, CMP_HIDDEN, Dh), CMP_HIDDEN ** -0.5),
        "cmp_k_b2": nrm(ks[14], (L, Dh), 0.02),
        "cmp_v_w1": nrm(ks[15], (L, CMP_BLOCK * Dh, CMP_HIDDEN), (CMP_BLOCK * Dh) ** -0.5),
        "cmp_v_b1": nrm(ks[16], (L, CMP_HIDDEN), 0.02),
        "cmp_v_w2": nrm(ks[17], (L, CMP_HIDDEN, Dh), CMP_HIDDEN ** -0.5),
        "cmp_v_b2": nrm(ks[18], (L, Dh), 0.02),
        "w_out": nrm(ks[19], (L, MIX_WIDTH, D_MODEL), MIX_WIDTH ** -0.5),
        "ffn_norm_g": 1.0 + nrm(ks[20], (L, D_MODEL), 0.02),
        "dense_w1": nrm(ks[21], (N_DENSE, D_MODEL, D_FF), D_MODEL ** -0.5),
        "dense_w3": nrm(ks[22], (N_DENSE, D_MODEL, D_FF), D_MODEL ** -0.5),
        "dense_w2": nrm(ks[23], (N_DENSE, D_FF, D_MODEL), D_FF ** -0.5),
        "router_w": nrm(ks[24], (N_MOE, D_MODEL, N_EXPERTS), D_MODEL ** -0.5),
        "moe_w1": nrm(ks[25], (N_MOE, N_EXPERTS, D_MODEL, D_FF_EXPERT), D_MODEL ** -0.5),
        "moe_w3": nrm(ks[26], (N_MOE, N_EXPERTS, D_MODEL, D_FF_EXPERT), D_MODEL ** -0.5),
        "moe_w2": nrm(ks[27], (N_MOE, N_EXPERTS, D_FF_EXPERT, D_MODEL), D_FF_EXPERT ** -0.5),
    }

def reference(x, attn_norm_g, w_in, conv_dw_w, conv_dw_b, conv_ln_g, conv_ln_b, q_norm_g, k_norm_g,
              cmp_pos_k, cmp_pos_v, cmp_k_w1, cmp_k_b1, cmp_k_w2, cmp_k_b2,
              cmp_v_w1, cmp_v_b1, cmp_v_w2, cmp_v_b2, w_out, ffn_norm_g,
              dense_w1, dense_w3, dense_w2, router_w, moe_w1, moe_w3, moe_w2):
    sizes = [CONV_WIDTH, CONV_WIDTH, ATTN_WIDTH] + [KV_WIDTH] * 6 + [N_HEADS * N_BRANCH]
    offsets = [int(o) for o in np.cumsum(sizes)[:-1]]
    for layer in range(DEPTH):
        h = rms_norm(x, attn_norm_g[layer])
        z = h @ w_in[layer]
        c_val, c_gate, q, k_c, v_c, k_s, v_s, k_w, v_w, g_log = jnp.split(z, offsets, axis=-1)
        conv_out = conv_module(c_val, c_gate, conv_dw_w[layer], conv_dw_b[layer],
                               conv_ln_g[layer], conv_ln_b[layer])
        attn_out = nsa_attention(q, k_c, v_c, k_s, v_s, k_w, v_w, g_log,
                                 q_norm_g[layer], k_norm_g[layer], cmp_pos_k[layer], cmp_pos_v[layer],
                                 cmp_k_w1[layer], cmp_k_b1[layer], cmp_k_w2[layer], cmp_k_b2[layer],
                                 cmp_v_w1[layer], cmp_v_b1[layer], cmp_v_w2[layer], cmp_v_b2[layer])
        x = x + jnp.concatenate([conv_out, attn_out], axis=-1) @ w_out[layer]
        h = rms_norm(x, ffn_norm_g[layer])
        if layer % 2 == 0:
            i = layer // 2
            x = x + swiglu(h, dense_w1[i], dense_w3[i], dense_w2[i])
        else:
            i = layer // 2
            x = x + moe_swiglu(h, router_w[i], moe_w1[i], moe_w3[i], moe_w2[i])
    return x


_drawn_inputs = setup_inputs


def setup_inputs(seed=0):
    import zlib

    import numpy as np

    out = dict(_drawn_inputs(seed))
    spreads = {}
    factors = {'q_norm_g': 2.689,
     'k_norm_g': 4.149,
     'cmp_pos_k': 3.113,
     'cmp_k_b1': 8.0,
     'cmp_k_b2': 6.557,
     'cmp_v_b1': 2.822,
     'cmp_v_b2': 3.737}
    for name, (base, spread) in spreads.items():
        noise = np.random.default_rng([zlib.crc32(name.encode()), seed]).standard_normal(out[name].shape)
        drawn = base * np.exp(spread * noise) if base else spread * noise
        out[name] = __import__('jax').numpy.asarray(drawn.astype(out[name].dtype))
    for name, factor in factors.items():
        out[name] = (out[name] * factor).astype(out[name].dtype)
    return out
```

```python
from contextlib import ExitStack

import concourse.bass as bass
from concourse import mybir

P = 128
BANK = 512
ALU = mybir.AluOpType
ACT = mybir.ActivationFunctionType
F32 = mybir.dt.float32
I32 = mybir.dt.int32
AX_X = mybir.AxisListType.X
NEG = -1e30
EPS = 1e-6


def hymba_trunk(nc, x, w_in, cmp_k_w1, cmp_v_w1, w_out, dense_w1, dense_w3, dense_w2,
                moe_w1, moe_w3, moe_w2, small, rows, router, out):
    S, D = x.shape
    L = w_in.shape[0]
    CONV = w_out.shape[1] // 2
    HD, KV, G = 64, 2, 4
    H = KV * G
    TAPS = 31
    CMP_BLOCK, CMP_STRIDE = 32, 16
    NCMP = (S - CMP_BLOCK) // CMP_STRIDE + 1
    CPAD = 32
    MC = CPAD + NCMP
    HID = cmp_k_w1.shape[2]
    FD = dense_w1.shape[1]
    E, FE = moe_w1.shape[0], moe_w1.shape[2]
    NT = S // P
    KD = D // P
    NH = D // BANK
    CC = CONV // P
    LP = CMP_BLOCK * HD // P
    ZA = w_in.shape[2] - 2 * CONV
    AW = H * HD
    KC0, VC0, KS0, VS0, KW0, VW0, GL0 = [AW + i * KV * HD for i in range(7)]
    PAD = TAPS - 1
    CAP = P
    PASSES = S // CAP
    FCH = FE // BANK
    FB = BANK // P
    DCH = [min(BANK, FD - c) for c in range(0, FD, BANK)]
    DFB = FD // P
    assert NT == 2 and NH == 2 and S <= 512 and FE % BANK == 0 and FD % P == 0 and L == 2

    sizes = [("attn_g", KD), ("ffn_g", KD), ("conv_w", CC * TAPS), ("conv_b", CC), ("ln_g", CC), ("ln_b", CC),
             ("q_g", 1), ("k_g", 3), ("pos", 2 * LP), ("w2", 2 * (HID // P) * HD)]
    col, at = {}, 0
    for name, n in sizes:
        col[name] = at
        at += n
    NSM = at
    assert small.shape[2] == NSM

    SLOTS, SLOT = 7, 8 * BANK
    stream = []
    for l in range(L):
        stream += [("win", l, c) for c in range(5)] + [("cmp", l, 0), ("cmp", l, 1)]
        stream += [("wout", l, 0), ("wout", l, 1)]
        if l == 0:
            for c in range(len(DCH)):
                stream += [("d1", l, c), ("d3", l, c), ("d2", l, c)]
    BASE = len(stream)
    place = {key: n for n, key in enumerate(stream)}
    expert_stream = [("e1", 0), ("e3", 0)]
    for c in range(1, FCH):
        expert_stream += [("e1", c), ("e3", c), ("e2", c - 1)]
    expert_stream += [("e2", FCH - 1)]
    XS = len(expert_stream)
    xplace = {key: m for m, key in enumerate(expert_stream)}
    assert XS % SLOTS == 0

    ctx = ExitStack()
    with ctx:
        def sb(name, shape, dt=F32):
            return ctx.enter_context(nc.sbuf_tensor(name, shape, dt))

        def sem(name):
            return ctx.enter_context(nc.semaphore(name))

        ring = sb("ring", [P, SLOTS, SLOT])
        x_sb = sb("x_sb", [P, NT, D])
        hn = sb("hn", [P, NT, D])
        hT = sb("hT", [P, KD, S])
        mixT = sb("mixT", [P, KD, S])
        par = sb("par", [P, L, NSM])
        rows_sb = sb("rows_sb", [33, rows.shape[1]])
        router_sb = sb("router_sb", [P, KD, E])
        ident = sb("ident", [P, P])
        before = sb("before", [P, P])
        ones = sb("ones", [P, P])
        group_mean = sb("group_mean", [P, P])
        iota_f = sb("iota_f", [P, P])
        causal = sb("causal", [P, 2 * P])
        cmask = sb("cmask", [P, NT, NCMP])
        cneg = sb("cneg", [P, NT, NCMP])
        minus_half = sb("minus_half", [P, 24])
        ss = sb("ss", [P, 2])
        rms = sb("rms", [P, 2])
        stat = sb("stat", [P, 24])
        rstat = sb("rstat", [P, 24])
        cstat = sb("cstat", [P, 2])
        gates = sb("gates", [P, NT, 24])
        negmax = sb("negmax", [P, 2, G])
        psumr = sb("psumr", [P, 2, G])
        pscale = sb("pscale", [P, 2, G])
        cmx = sb("cmx", [P, NT * H])
        csum = sb("csum", [P, NT * H])
        crs = sb("crs", [P, NT * H])
        rt = sb("rt", [P, 16, NT, E])
        rv = sb("rv", [P, 8, NT])
        eidx = sb("eidx", [P, NT, E])
        pos_tab = sb("pos_tab", [P, NT, PASSES * E + 1])
        wgt_tab = sb("wgt_tab", [P, NT, PASSES * E + 1])
        mcount = sb("mcount", [P, 2])
        trips_i = sb("trips_i", [P, 1], I32)

        ARENA = 11944
        arena = sb("arena", [P, ARENA])

        def carve(sizes):
            at, got = 0, []
            for n in sizes:
                got.append(arena[:, at:at + n])
                at += n
            assert at <= ARENA, at
            return got

        z_, qT_, kT_, pt_, u_, y_, sq_, sig_ = carve(
            [NT * ZA, G * S, 2 * S, 2 * 4 * BANK, CC * (PAD + S), CC * S, 2 * BANK, 2 * S])
        z = z_.rearrange("p (i c) -> p i c", i=NT)
        qT = qT_.rearrange("p (g t) -> p g t", g=G)
        kT = kT_.rearrange("p (b t) -> p b t", b=2)
        probsT = pt_.rearrange("p (w b k n) -> p w b k n", w=2, b=2, k=2)
        u = u_.rearrange("p (c t) -> p c t", c=CC)
        y = y_.rearrange("p (c t) -> p c t", c=CC)
        sq = sq_
        sig = sig_.rearrange("p (b t) -> p b t", b=2)
        zdup = pt_[:, 0:NT * 4 * P].rearrange("p (i a e d) -> p i a e d", i=NT, a=4, e=2)
        hid = pt_[:, 1024:1024 + 2 * HID].rearrange("p (a n) -> p a n", a=2)
        hidT = pt_[:, 1536:1536 + 4 * CPAD * 2].rearrange("p (a n) -> p a n", a=4)
        blkT = pt_[:, 2048:2048 + 2 * LP * 2 * CPAD].rearrange("p (a l m) -> p a l m", a=2, l=LP)
        hn_flat = hn[:].rearrange("p i d -> p (i d)")
        qn = hn_flat[:, 0:NT * AW].rearrange("p (i g k d) -> p i g k d", i=NT, g=G, k=KV)
        kn = hn_flat[:, NT * AW:NT * AW + NT * 2 * P].rearrange("p (i b k d) -> p i b k d", i=NT, b=2, k=KV)
        scores = hn_flat[:, 0:2 * BANK].rearrange("p (a n) -> p a n", a=2)
        probs = hn_flat[:, 2 * BANK:4 * BANK].rearrange("p (a n) -> p a n", a=2)
        cp = sb("cp", [P, NT, G, KV, CPAD])
        cpT = sq_[:, 0:NT * BANK].rearrange("p (i n) -> p i n", i=NT)
        kcn = sb("kcn", [P, 2, HD])
        kcT = sb("kcT", [P, MC])
        vc = sb("vc", [P, HD])
        xeT_, sg_, act_, actT_, ye, sel_, wsel_, wselT = carve(
            [KD * CAP, 2 * BANK, 2 * BANK, 2 * BANK, D, NT * CAP, NT * CAP, S])
        xeT = xeT_.rearrange("p (k s) -> p k s", k=KD)
        sg = sg_.rearrange("p (a n) -> p a n", a=2)
        act = act_.rearrange("p (a n) -> p a n", a=2)
        actT = actT_.rearrange("p (a n) -> p a n", a=2)
        sel = sel_.rearrange("p (i s) -> p i s", i=NT)
        wsel = wsel_.rearrange("p (i s) -> p i s", i=NT)
        dsg = sg_.rearrange("p (a n) -> p a n", a=4)
        dactT = act_.rearrange("p (a n) -> p a n", a=4)

        bank = [ctx.enter_context(nc.psum_tensor(f"bank{b}", [P, BANK], F32)) for b in range(8)]

        x_loaded, par_loaded = sem("x_loaded"), sem("par_loaded")
        arrived = [sem(f"slot{s}_arrived") for s in range(SLOTS)]
        const_step, const_ready = sem("const_step"), sem("const_ready")
        pads_ready = sem("pads_ready")
        ss_ready, ms_ready, rms_ready, hn_ready = sem("ss_ready"), sem("ms_ready"), sem("rms_ready"), sem("hn_ready")
        hT_psum, hT_ready = sem("hT_psum"), sem("hT_ready")
        glu_psum, sig_ready, u_ready, conv_step = sem("glu_psum"), sem("sig_ready"), sem("u_ready"), sem("conv_step")
        conv_done = sem("conv_done")
        z_psum, z_ready = sem("z_psum"), sem("z_ready")
        zdup_ready, zdup_psum, blk_ready = sem("zdup_ready"), sem("zdup_psum"), sem("blk_ready")
        hid_psum, hid_ready, hidT_psum, hidT_ready = sem("hid_psum"), sem("hid_ready"), sem("hidT_psum"), sem("hidT_ready")
        cmp_psum, vc_ready, kcn_ready, kcT_psum, kcT_ready = (
            sem("cmp_psum"), sem("vc_ready"), sem("kcn_ready"), sem("kcT_psum"), sem("kcT_ready"))
        stat_ready, rstat_ready, cstat_ready, rcstat_ready = (
            sem("stat_ready"), sem("rstat_ready"), sem("cstat_ready"), sem("rcstat_ready"))
        qkn_ready, qkT_psum, qkT_ready = sem("qkn_ready"), sem("qkT_psum"), sem("qkT_ready")
        cs_psum, cs_ready, cexp_ready, cp_ready, cpT_psum, cpT_ready = (
            sem("cs_psum"), sem("cs_ready"), sem("cexp_ready"), sem("cp_ready"), sem("cpT_psum"), sem("cpT_ready"))
        gates_ready = sem("gates_ready")
        s_psum, s_ready, exp_ready, p_ready, pT_psum, pT_ready = (
            sem("s_psum"), sem("s_ready"), sem("exp_ready"), sem("p_ready"), sem("pT_psum"), sem("pT_ready"))
        o_psum, mix_ready = sem("o_psum"), sem("mix_ready")
        mean_psum, centred_ready, var_psum, var_ready, std_ready, yn_ready, conv_mix = (
            sem("mean_psum"), sem("centred_ready"), sem("var_psum"), sem("var_ready"), sem("std_ready"),
            sem("yn_ready"), sem("conv_mix"))
        wo_psum, x_ready = sem("wo_psum"), sem("x_ready")
        ffn_psum, dsg_ready, dact_ready, ffn_down, dense_psum = (
            sem("ffn_psum"), sem("dsg_ready"), sem("dact_ready"), sem("ffn_down"), sem("dense_psum"))
        dve_step, act_step = sem("dve_step"), sem("act_step")
        logit_psum, lse_ready, lexp_ready, chosen_ready, pos_psum, trips_ready = (
            sem("logit_psum"), sem("lse_ready"), sem("lexp_ready"), sem("chosen_ready"), sem("pos_psum"),
            sem("trips_ready"))
        h1_full, h3_full, sg_ready, act_ready, down_done, y_drained = (
            sem("h1_full"), sem("h3_full"), sem("sg_ready"), sem("act_ready"), sem("down_done"), sem("y_drained"))
        b7_full, b7_drained, b4_full, b4_drained = (
            sem("b7_full"), sem("b7_drained"), sem("b4_full"), sem("b4_drained"))
        sel_ready, wsel_ready = sem("sel_ready"), sem("wsel_ready")
        trips_done, stored = sem("trips_done"), sem("stored")

        def slot(n):
            return ring[:, n % SLOTS, :]

        def source(kind, l, c):
            if kind == "win":
                n = min(BANK, w_in.shape[2] - c * BANK)
                return w_in[l, :, c * BANK:c * BANK + n].rearrange("(k p) n -> p k n", p=P), KD, n
            if kind == "cmp":
                w = (cmp_k_w1, cmp_v_w1)[c]
                return w[l].rearrange("(k p) n -> p k n", p=P), LP, HID
            if kind == "wout":
                return w_out[l, :, c * BANK:(c + 1) * BANK].rearrange("(k p) n -> p k n", p=P), KD, BANK
            n = DCH[c]
            if kind == "d2":
                return dense_w2[c * BANK:c * BANK + n, :].rearrange("(k p) n -> p k n", p=P), n // P, D
            w = dense_w1 if kind == "d1" else dense_w3
            return w[:, c * BANK:c * BANK + n].rearrange("(k p) n -> p k n", p=P), KD, n

        def view(kind, l, c):
            _, k, n = source(kind, l, c)
            return slot(place[kind, l, c])[:, 0:k * n].rearrange("p (k n) -> p k n", k=k)

        def expert_view(kind, c):
            s = slot(BASE + xplace[kind, c])
            return s.rearrange("p (k n) -> p k n", k=(FB if kind == "e2" else KD))

        def dense_blocks(c):
            return sum(DCH[:c + 1]) // P

        def last_read(n):
            kind, l, c = stream[n]
            return {"win": (glu_psum, CC * (l + 1)) if c < 2 else (z_psum, 6 * l + 2 * (c - 1)),
                    "cmp": (hid_psum, 2 * l + c + 1),
                    "wout": (wo_psum, 2 * NT * l + NT * (c + 1)),
                    "d1": (ffn_psum, dense_blocks(c) if l == 0 and kind[0] == "d" else 0),
                    "d3": (ffn_psum, dense_blocks(c) if l == 0 and kind[0] == "d" else 0),
                    "d2": (ffn_down, dense_blocks(c) if l == 0 and kind[0] == "d" else 0)}[kind]

        def wait_static(eng, kind, l, c):
            n = place[kind, l, c]
            eng.wait_ge(arrived[n % SLOTS], 16 * (n // SLOTS + 1))

        def wait_expert(eng, kind, c, j):
            n = BASE + xplace[kind, c]
            eng.wait_ge(arrived[n % SLOTS], j * (16 * XS // SLOTS) + 16 * (n // SLOTS + 1))

        units = []
        groups = [(kv, i) for i in range(NT) for kv in range(KV)]
        for gi, (kv, i) in enumerate(groups):
            for b in range(2):
                for h0 in range(0, G, G // (i + 1)):
                    units.append((gi, kv, i, b, h0, G // (i + 1)))
        NU = len(units)
        group_last = [max(n for n, un in enumerate(units) if un[0] == gi) for gi in range(len(groups))]

        def exp_count(l, n):
            return l * sum(un[5] for un in units) + sum(un[5] for un in units[:n + 1])

        block = ctx.enter_context(nc.Block())

        @block.sync
        def _(sp):
            for i in range(NT):
                sp.dma_start(x_sb[:, i, :], x[i * P:(i + 1) * P, :]).then_inc(x_loaded, 16)
            for n, key in enumerate(stream):
                if n >= SLOTS:
                    sp.wait_ge(*last_read(n - SLOTS))
                src, k, m = source(*key)
                sp.dma_start(slot(n)[:, 0:k * m].rearrange("p (k n) -> p k n", k=k), src) \
                    .then_inc(arrived[n % SLOTS], 16)

            def read_count(kind):
                return {"e1": h1_full, "e3": h3_full, "e2": down_done}[kind]

            def stream_expert(j, e, first):
                w1 = moe_w1[e].rearrange("(k p) n -> p k n", p=P)
                w3 = moe_w3[e].rearrange("(k p) n -> p k n", p=P)
                w2 = moe_w2[e].rearrange("(k p) n -> p k n", p=P)
                for m, (kind, c) in enumerate(expert_stream):
                    if m >= SLOTS:
                        pkind, pc = expert_stream[m - SLOTS]
                        sp.wait_ge(read_count(pkind), j * FCH + pc + 1)
                    elif first:
                        sp.wait_ge(*last_read(BASE + m - SLOTS))
                    else:
                        pkind, pc = expert_stream[XS + m - SLOTS]
                        sp.wait_ge(read_count(pkind), j * FCH + (pc + 1 - FCH))
                    dst = expert_view(kind, c)
                    if kind == "e2":
                        src = w2[:, c * FB:(c + 1) * FB, :]
                    else:
                        src = (w1 if kind == "e1" else w3)[:, :, c * BANK:(c + 1) * BANK]
                    sp.dma_start(dst, src).then_inc(arrived[(BASE + m) % SLOTS], 16)

            stream_expert(0, 0, True)
            with sp.Fori(1, E) as j:
                stream_expert(j, j, False)
            sp.wait_ge(trips_ready, 1)
            trips = sp.value_load(trips_i[0:1, 0:1], min_val=E, max_val=PASSES * E)
            with sp.If(trips > E):
                with sp.Fori(E, PASSES * E) as j:
                    stream_expert(j, j - E, False)
            sp.wait_ge(trips_done, 1)
            for i in range(NT):
                sp.dma_start(out[i * P:(i + 1) * P, :], x_sb[:, i, :]).then_inc(stored, 16)
            sp.wait_ge(stored, 16 * NT)

        @block.gpsimd
        def _(pl):
            nc.gpsimd.memset(ident[:], 0.0).then_inc(const_step, 1)
            nc.gpsimd.memset(ones[:], 1.0).then_inc(const_step, 1)
            nc.gpsimd.memset(causal[:], 0.0).then_inc(const_step, 1)
            nc.gpsimd.memset(cmask[:], 1.0).then_inc(const_step, 1)
            nc.gpsimd.memset(cneg[:], 0.0).then_inc(const_step, 1)
            nc.gpsimd.memset(group_mean[:], 1.0 / HD).then_inc(const_step, 1)
            nc.gpsimd.memset(minus_half[:], -0.5).then_inc(const_step, 1)
            nc.gpsimd.memset(before[:], 1.0).then_inc(const_step, 1)
            nc.gpsimd.iota(iota_f[:], pattern=[[1, P]], base=0, channel_multiplier=0,
                           allow_small_or_imprecise_dtypes=True).then_inc(const_step, 1)
            nc.gpsimd.iota(eidx[:], pattern=[[0, NT], [1, E]], base=0, channel_multiplier=0,
                           allow_small_or_imprecise_dtypes=True).then_inc(const_step, 1)
            pl.wait_ge(const_step, 10)
            nc.gpsimd.affine_select(out=ident[:], in_=ident[:], compare_op=ALU.not_equal, fill=1.0, base=0,
                                    pattern=[[-1, P]], channel_multiplier=1).then_inc(const_ready, 1)
            nc.gpsimd.affine_select(out=causal[:, P:], in_=causal[:, P:], compare_op=ALU.is_ge, fill=NEG, base=0,
                                    pattern=[[-1, P]], channel_multiplier=1).then_inc(const_ready, 1)
            for m, fill in ((cmask, 0.0), (cneg, NEG)):
                nc.gpsimd.affine_select(out=m[:], in_=m[:], compare_op=ALU.is_ge, fill=fill,
                                        base=-(CMP_BLOCK - 1), pattern=[[P, NT], [-CMP_STRIDE, NCMP]],
                                        channel_multiplier=1).then_inc(const_ready, 1)
            nc.gpsimd.affine_select(out=before[:], in_=before[:], compare_op=ALU.is_ge, fill=0.0, base=-1,
                                    pattern=[[1, P]], channel_multiplier=-1).then_inc(const_ready, 1)
            for n, p0 in enumerate((0, HD)):
                pl.wait_ge(const_ready, 5 + n)
                blk = group_mean[p0:p0 + HD, HD - p0:2 * HD - p0]
                nc.gpsimd.memset(blk, 0.0).then_inc(const_ready, 1)
            pl.wait_ge(const_ready, 7)
            nc.gpsimd.memset(u[:, :, 0:PAD], 0.0).then_inc(pads_ready, 1)
            nc.gpsimd.memset(cp[:], 0.0).then_inc(pads_ready, 1)

            for l in range(L):
                for m in (2 * l, 2 * l + 1):
                    if m % 2 == 0:
                        pl.wait_ge(ms_ready, m + 1)
                        nc.gpsimd.tensor_tensor(rms[:], ss[:], minus_half[:, 0:NT], ALU.pow).then_inc(rms_ready, 1)
                        pl.wait_ge(stat_ready, l + 1)
                        nc.gpsimd.tensor_tensor(rstat[:], stat[:], minus_half[:], ALU.pow).then_inc(rstat_ready, 1)
                        pl.wait_ge(rstat_ready, l + 1)
                        pl.wait_ge(cstat_ready, l + 1)
                        nc.gpsimd.tensor_tensor(cstat[0:MC, 1:2], cstat[0:MC, 0:1], minus_half[0:MC, 0:1],
                                                ALU.pow).then_inc(rcstat_ready, 1)
                    else:
                        pl.wait_ge(rcstat_ready, l + 1)
                        pl.wait_ge(ms_ready, m + 1)
                        nc.gpsimd.tensor_tensor(rms[:], ss[:], minus_half[:, 0:NT], ALU.pow).then_inc(rms_ready, 1)

        @block.scalar
        def _(sc):
            sc.dma_start(par[:], small.rearrange("l p n -> p l n")).then_inc(par_loaded, 16)
            sc.dma_start(rows_sb[0:33:32, :], rows[:, :]).then_inc(par_loaded, 16)
            sc.dma_start(router_sb[:], router.rearrange("(k p) e -> p k e", p=P)).then_inc(par_loaded, 16)
            sc.wait_ge(par_loaded, 48)

            def p_(l, name, i=0, n=1):
                return par[:, l, col[name] + i:col[name] + i + n]

            def square_sums(m):
                if m == 0:
                    sc.wait_ge(x_loaded, 16 * NT)
                else:
                    sc.wait_ge(x_ready, 4 * m)
                for i in range(NT):
                    nc.scalar.activation(hn[:, i, :], x_sb[:, i, :], ACT.Square,
                                         accum_out=ss[:, i:i + 1]).then_inc(ss_ready, 1)

            for l in range(L):
                square_sums(2 * l)
                for c in range(CC):
                    sc.wait_ge(glu_psum, CC * l + c + 1)
                    if c >= 2:
                        sc.wait_ge(u_ready, CC * l + c - 1)
                    nc.scalar.activation(sig[:, c % 2, :], bank[c % 2][:, S:2 * S], ACT.Sigmoid).then_inc(sig_ready, 1)
                for n in range(6):
                    c, i = divmod(n, NT)
                    w = min(BANK, ZA - c * BANK)
                    sc.wait_ge(z_psum, 6 * l + n + 1)
                    nc.scalar.copy(z[:, i, c * BANK:c * BANK + w], bank[2 + n][:, 0:w]).then_inc(z_ready, 1)
                sc.wait_ge(z_ready, 6 * l + 6)
                for i in range(NT):
                    nc.scalar.activation(gates[:, i, :], z[:, i, GL0:GL0 + 3 * H], ACT.Sigmoid).then_inc(gates_ready, 1)
                for a in range(2):
                    sc.wait_ge(hid_psum, 2 * l + a + 1)
                    nc.scalar.activation(hid[0:MC, a, :], bank[5 + a][0:MC, 0:HID], ACT.Silu).then_inc(hid_ready, 1)
                sc.wait_ge(hidT_psum, l + 1)
                nc.scalar.copy(hidT[:, :, 0:MC],
                               bank[7][:, 0:4 * 2 * CPAD].rearrange("p (a n) -> p a n", a=4)[:, :, 0:MC]) \
                    .then_inc(hidT_ready, 1)
                sc.wait_ge(cmp_psum, 2 * l + 2)
                nc.scalar.copy(vc[0:MC, :], bank[6][0:MC, 0:HD]).then_inc(vc_ready, 1)
                sc.wait_ge(cs_ready, l + 1)
                for i in range(NT):
                    nc.scalar.activation(cp[:, i, :, :, 0:NCMP], cp[:, i, :, :, 0:NCMP], ACT.Exp).then_inc(cexp_ready, 1)

                def evacuate_cpT():
                    sc.wait_ge(cpT_psum, l + 1)
                    for i in range(NT):
                        nc.scalar.copy(cpT[0:2 * CPAD, i, :], bank[6 + i][0:2 * CPAD, :]).then_inc(cpT_ready, 1)

                def evacuate_pT(n):
                    gi, kv, i, b, h0, nh = units[n]
                    sc.wait_ge(pT_psum, NU * l + n + 1)
                    if gi >= 2:
                        sc.wait_ge(o_psum, 4 * l + gi - 1)
                    dst = probsT[:, gi % 2, b, 0:i + 1, h0 * P:(h0 + nh) * P]
                    src = bank[2 + n % 2][:].rearrange("p (k n) -> p k n", k=i + 1)
                    nc.scalar.copy(dst, src).then_inc(pT_ready, 1)

                def evacuate_o(gi):
                    kv, i = groups[gi]
                    sc.wait_ge(o_psum, 4 * l + gi + 1)
                    r = slice(kv * HD, (kv + 1) * HD)
                    nc.scalar.copy(mixT[r, CC:CC + G, i * P:(i + 1) * P],
                                   bank[4 + i][r, :].rearrange("p (g t) -> p g t", g=G)).then_inc(mix_ready, 1)

                for n in range(NU + 1):
                    if n < NU:
                        gi, kv, i, b, h0, nh = units[n]
                        keys = (i + 1) * P
                        sc.wait_ge(s_ready, NU * l + n + 1)
                        if n >= 2:
                            sc.wait_ge(pT_psum, NU * l + n - 1)
                        for h in range(nh):
                            nc.scalar.activation(probs[:, n % 2, h * keys:(h + 1) * keys],
                                                 scores[:, n % 2, h * keys:(h + 1) * keys], ACT.Exp,
                                                 bias=negmax[:, n % 2, h:h + 1],
                                                 accum_out=psumr[:, n % 2, h:h + 1]).then_inc(exp_ready, 1)
                    if n == 0:
                        evacuate_cpT()
                    if n >= 1:
                        evacuate_pT(n - 1)
                        for gi in range(len(groups)):
                            if n - 1 == group_last[gi] + 1:
                                evacuate_o(gi)
                evacuate_o(len(groups) - 1)
                sc.wait_ge(var_ready, 2 * (l + 1))
                nc.scalar.activation(sq[:, 0:CC * S], sq[:, 0:CC * S], ACT.Sqrt).then_inc(std_ready, 1)
                sc.wait_ge(yn_ready, l + 1)
                for c in range(CC):
                    nc.scalar.activation(mixT[:, c, :], y[:, c, :], ACT.Silu, scale=p_(l, "ln_g", c),
                                         bias=p_(l, "ln_b", c)).then_inc(conv_mix, 1)
                square_sums(2 * l + 1)
                if l == 0:
                    for f in range(DFB):
                        sc.wait_ge(ffn_psum, f + 1)
                        if f >= 4:
                            sc.wait_ge(dact_ready, f - 3)
                        nc.scalar.activation(dsg[:, f % 4, :], bank[4 + f % 4][:, 0:S], ACT.Silu).then_inc(dsg_ready, 1)

            sc.wait_ge(lse_ready, 1)
            nc.scalar.activation(rv[:, 3, :], rv[:, 2, :], ACT.Exp).then_inc(lexp_ready, 1)
            nc.scalar.copy(ss[:, 0:1], rms[:, 0:1]).then_inc(y_drained, 1)

            sc.wait_ge(trips_ready, 1)
            trips = sc.value_load(trips_i[0:1, 0:1], min_val=E, max_val=PASSES * E)
            with sc.Fori(0, trips) as j:
                def gate_silu(c):
                    sc.wait_ge(h1_full, j * FCH + c + 1)
                    sc.wait_ge(act_ready, j * FCH + max(c - 1, 0) + 1)
                    nc.scalar.activation(sg[:, c % 2, :], bank[c % 2][:], ACT.Silu).then_inc(sg_ready, 1)

                def drain_transposes(c):
                    sc.wait_ge(b4_full, j * (FCH + 2) + c + 1)
                    if c >= 2:
                        sc.wait_ge(down_done, j * FCH + c - 1)
                    nc.scalar.copy(actT[:, c % 2, :], bank[4][:]).then_inc(b4_drained, 1)

                gate_silu(0)
                for c in range(1, FCH):
                    gate_silu(c)
                    drain_transposes(c - 1)
                    if c == 3:
                        sc.wait_ge(b7_full, j * 5 + 3)
                        nc.scalar.copy(wselT[:], bank[7][:, 0:S]).then_inc(b7_drained, 1)
                drain_transposes(FCH - 1)
                sc.wait_ge(down_done, (j + 1) * FCH)
                for n in range(NH):
                    nc.scalar.copy(ye[:, n * BANK:(n + 1) * BANK], bank[5 + n][:]).then_inc(y_drained, 1)

        @block.vector
        def _(dv):
            steps = [0]

            def link(ins):
                steps[0] += 1
                ins.then_inc(dve_step, 1)
                dv.wait_ge(dve_step, steps[0])

            V = nc.vector

            def p_(l, name, i=0, n=1):
                return par[:, l, col[name] + i:col[name] + i + n]

            dv.wait_ge(par_loaded, 48)
            dv.wait_ge(const_ready, 7)
            dv.wait_ge(pads_ready, 2)

            def normalise(m):
                l, ffn = divmod(m, 2)
                dv.wait_ge(ss_ready, NT * (m + 1))
                V.tensor_scalar(ss[:], ss[:], 1.0 / D, EPS, ALU.mult, ALU.add).then_inc(ms_ready, 1)
                dv.wait_ge(rms_ready, m + 1)
                for i in range(NT):
                    V.tensor_scalar(hn[:, i, :], x_sb[:, i, :], rms[:, i:i + 1], None, ALU.mult).then_inc(hn_ready, 1)
                gain = p_(l, "ffn_g" if ffn else "attn_g", 0, KD)
                for q in range(4):
                    i, h = divmod(q, 2)
                    dv.wait_ge(hT_psum, 4 * m + q + 1)
                    V.tensor_tensor(hT[:, 4 * h:4 * h + 4, i * P:(i + 1) * P],
                                    bank[4 + q][:].rearrange("p (k t) -> p k t", k=4),
                                    gain[:, 4 * h:4 * h + 4].unsqueeze(2).to_broadcast([P, 4, P]),
                                    ALU.mult).then_inc(hT_ready, 1)

            def add_to_x(b, i, n):
                part = x_sb[:, i, n * BANK:(n + 1) * BANK]
                return V.tensor_tensor(part, part, bank[b][:], ALU.add)

            conv_n = [0]

            for l in range(L):
                normalise(2 * l)

                def glu(c):
                    dv.wait_ge(sig_ready, CC * l + c + 1)
                    V.tensor_tensor(u[:, c, PAD:], bank[c % 2][:, 0:S], sig[:, c % 2, :], ALU.mult).then_inc(u_ready, 1)

                for c0 in range(0, CC, 2):
                    if c0 == 0:
                        glu(0)
                        glu(1)
                    dv.wait_ge(u_ready, CC * l + c0 + 2)
                    for tap in range(TAPS):
                        for c in (c0, c0 + 1):
                            w = p_(l, "conv_w", c * TAPS + tap)
                            if tap == 0:
                                V.tensor_scalar(y[:, c, :], u[:, c, 0:S], w, p_(l, "conv_b", c), ALU.mult,
                                                ALU.add).then_inc(conv_step, 1)
                            else:
                                dv.wait_ge(conv_step, conv_n[0] - 1)
                                V.scalar_tensor_tensor(out=y[:, c, :], in0=u[:, c, tap:tap + S], scalar=w,
                                                       in1=y[:, c, :], op0=ALU.mult,
                                                       op1=ALU.add).then_inc(conv_step, 1)
                            conv_n[0] += 1
                        if c0 == 0 and tap in (8, 16):
                            glu(2 if tap == 8 else 3)

                dv.wait_ge(z_ready, 6 * (l + 1))
                for i in range(NT):
                    zq = z[:, i, 0:AW]
                    link(V.tensor_tensor(sq[:, 0:AW], zq, zq, ALU.mult))
                    zk = z[:, i, KS0:KS0 + 4 * P].rearrange("p (b c) -> p b c", b=2)[:, :, 0:P]
                    link(V.tensor_tensor(sq[:, AW:AW + 2 * P].rearrange("p (b c) -> p b c", b=2), zk, zk, ALU.mult))
                    link(V.tensor_reduce(stat[:, i * 12:(i + 1) * 12],
                                         sq[:, 0:AW + 2 * P].rearrange("p (h d) -> p h d", d=HD), AX_X, ALU.add))
                V.tensor_scalar(stat[:], stat[:], 1.0 / HD, EPS, ALU.mult, ALU.add).then_inc(stat_ready, 1)
                for i in range(NT):
                    src = z[:, i, KC0:KC0 + 4 * HD].rearrange("p (a d) -> p a d", a=4)
                    V.tensor_copy(zdup[:, i], src.unsqueeze(2).to_broadcast([P, 4, 2, HD])).then_inc(zdup_ready, 1)
                dv.wait_ge(rstat_ready, l + 1)
                for i in range(NT):
                    rs = rstat[:, i * 12:i * 12 + 8].rearrange("p (k g) -> p k g", k=KV)
                    for kv in range(KV):
                        V.tensor_tensor(qn[:, i, :, kv, :],
                                        z[:, i, kv * G * HD:(kv + 1) * G * HD].rearrange("p (g d) -> p g d", g=G),
                                        rs[:, kv, :].unsqueeze(2).to_broadcast([P, G, HD]),
                                        ALU.mult).then_inc(qkn_ready, 1)
                    for b in range(2):
                        k0 = KS0 + b * 2 * P
                        V.tensor_tensor(kn[:, i, b], z[:, i, k0:k0 + P].rearrange("p (k d) -> p k d", k=KV),
                                        rstat[:, i * 12 + 8 + 2 * b:i * 12 + 10 + 2 * b].unsqueeze(2)
                                        .to_broadcast([P, KV, HD]), ALU.mult).then_inc(qkn_ready, 1)
                if l == 0:
                    link(V.memset(blkT[:], 0.0))
                else:
                    link(V.memset(blkT[:], 0.0))
                for a in range(2):
                    dv.wait_ge(zdup_psum, 2 * l + a + 1)
                    for kv in range(KV):
                        for q in range(2):
                            r = slice(q * HD, (q + 1) * HD)
                            src = bank[3 + a][r, kv * S:(kv + 1) * S].rearrange("p (c o e) -> p c o e", e=2, o=8)
                            for half in range(2):
                                dst = blkT[r, a, 8 * half:8 * half + 8, kv * CPAD:kv * CPAD + NCMP]
                                V.tensor_tensor(dst, src[:, half:half + NCMP, :, q].rearrange("p c o -> p o c"),
                                                par[r, l, col["pos"] + a * LP + 8 * half:
                                                    col["pos"] + a * LP + 8 * half + 8].unsqueeze(2)
                                                .to_broadcast([HD, 8, NCMP]), ALU.add).then_inc(blk_ready, 1)
                for i in range(NT):
                    dv.wait_ge(qkT_psum, 3 * l + i + 1)
                    V.tensor_scalar(qT[:, :, i * P:(i + 1) * P], bank[i][:].rearrange("p (g t) -> p g t", g=G),
                                    p_(l, "q_g"), HD ** -0.5, ALU.mult, ALU.mult).then_inc(qkT_ready, 1)
                dv.wait_ge(qkT_psum, 3 * l + 3)
                for b in range(2):
                    V.tensor_scalar(kT[:, b, :], bank[2][:, b * S:(b + 1) * S], p_(l, "k_g", 1 + b), None,
                                    ALU.mult).then_inc(qkT_ready, 1)

                def masked_scores(n):
                    gi, kv, i, b, h0, nh = units[n]
                    keys = (i + 1) * P
                    dv.wait_ge(s_psum, NU * l + n + 1)
                    if n >= 2:
                        dv.wait_ge(exp_ready, exp_count(l, n - 2))
                    s3 = scores[:, n % 2, :].rearrange("p (h k) -> p h k", h=nh)
                    link(V.tensor_tensor(s3, bank[n % 2][:].rearrange("p (h k) -> p h k", h=nh),
                                         causal[:, 2 * P - keys:].unsqueeze(1).to_broadcast([P, nh, keys]), ALU.add))
                    V.tensor_reduce(negmax[:, n % 2, 0:nh], s3, AX_X, ALU.max, negate=True).then_inc(s_ready, 1)

                dv.wait_ge(cmp_psum, 2 * l + 1)
                link(V.tensor_copy(kcn[0:MC, 0, :], bank[5][0:MC, 0:HD]))
                link(V.tensor_tensor(kcn[0:MC, 1, :], kcn[0:MC, 0, :], kcn[0:MC, 0, :], ALU.mult))
                link(V.tensor_reduce(cstat[0:MC, 0:1], kcn[0:MC, 1, :], AX_X, ALU.add))
                V.tensor_scalar(cstat[0:MC, 0:1], cstat[0:MC, 0:1], 1.0 / HD, EPS, ALU.mult, ALU.add) \
                    .then_inc(cstat_ready, 1)
                dv.wait_ge(rcstat_ready, l + 1)
                link(V.tensor_scalar(kcn[0:MC, 0, :], kcn[0:MC, 0, :], cstat[0:MC, 1:2], None, ALU.mult))
                V.tensor_copy(kcn[0:MC, 1, :], kcn[0:MC, 0, :]).then_inc(kcn_ready, 1)
                dv.wait_ge(kcT_psum, l + 1)
                V.tensor_scalar(kcT[:], bank[7][:, 0:MC], p_(l, "k_g", 0), None, ALU.mult).then_inc(kcT_ready, 1)
                dv.wait_ge(cs_psum, KV * (l + 1))
                cpv = cp[:].rearrange("p i g k c -> p i (g k) c")[:, :, :, 0:NCMP]
                cflat = cp[:].rearrange("p i g k c -> p (i g k) c")[:, :, 0:NCMP]
                for kv in range(KV):
                    cps = bank[6 + kv][:, 0:NT * G * CPAD].rearrange("p (i g c) -> p i g c", i=NT, g=G)
                    for i in range(NT):
                        link(V.tensor_tensor(cp[:, i, :, kv, 0:NCMP], cps[:, i, :, 0:NCMP],
                                             cneg[:, i, :].unsqueeze(1).to_broadcast([P, G, NCMP]), ALU.add))
                link(V.tensor_reduce(cmx[:], cflat, AX_X, ALU.max))
                V.tensor_tensor(cflat, cflat, cmx[:].unsqueeze(2).to_broadcast([P, NT * H, NCMP]),
                                ALU.subtract).then_inc(cs_ready, 1)
                masked_scores(0)
                dv.wait_ge(cexp_ready, NT * (l + 1))
                for i in range(NT):
                    link(V.tensor_tensor(cpv[:, i], cpv[:, i], cmask[:, i, :].unsqueeze(1).to_broadcast([P, H, NCMP]),
                                         ALU.mult))
                link(V.tensor_reduce(csum[:], cflat, AX_X, ALU.add))
                link(V.tensor_scalar(csum[:], csum[:], 1e-30, None, ALU.max))
                link(V.reciprocal(csum[:], csum[:]))
                dv.wait_ge(gates_ready, NT * (l + 1))
                for i in range(NT):
                    gv = gates[:, i, :].rearrange("p (k g b) -> p g k b", k=KV, g=G)[:, :, :, 0]
                    link(V.tensor_tensor(crs[:, i * H:(i + 1) * H].rearrange("p (g k) -> p g k", g=G),
                                         csum[:, i * H:(i + 1) * H].rearrange("p (g k) -> p g k", g=G), gv, ALU.mult))
                V.tensor_tensor(cflat, cflat, crs[:].unsqueeze(2).to_broadcast([P, NT * H, NCMP]),
                                ALU.mult).then_inc(cp_ready, 1)
                for n in range(NU):
                    if n + 1 < NU:
                        masked_scores(n + 1)
                    gi, kv, i, b, h0, nh = units[n]
                    keys = (i + 1) * P
                    dv.wait_ge(exp_ready, exp_count(l, n))
                    link(V.reciprocal(pscale[:, n % 2, 0:nh], psumr[:, n % 2, 0:nh]))
                    gv = gates[:, i, :].rearrange("p (h b) -> p h b", b=3)[:, kv * G + h0:kv * G + h0 + nh, 1 + b]
                    link(V.tensor_tensor(pscale[:, n % 2, 0:nh], pscale[:, n % 2, 0:nh], gv, ALU.mult))
                    p3 = probs[:, n % 2, :].rearrange("p (h k) -> p h k", h=nh)
                    V.tensor_tensor(p3, p3, pscale[:, n % 2, 0:nh].unsqueeze(2).to_broadcast([P, nh, keys]),
                                    ALU.mult).then_inc(p_ready, 1)

                for h in range(2):
                    dv.wait_ge(mean_psum, 2 * l + h + 1)
                    part = y[:, 2 * h:2 * h + 2, :]
                    V.tensor_tensor(part, part, bank[6 + h][:].rearrange("p (c t) -> p c t", c=2),
                                    ALU.subtract).then_inc(centred_ready, 1)
                dv.wait_ge(centred_ready, 3 * l + 2)
                dv.wait_ge(o_psum, 4 * (l + 1))
                yf = y[:].rearrange("p c t -> p (c t)")
                V.tensor_tensor(sq[:, 0:CC * S], yf, yf, ALU.mult).then_inc(centred_ready, 1)
                for h in range(2):
                    dv.wait_ge(var_psum, 2 * l + h + 1)
                    if h == 0:
                        dv.wait_ge(var_psum, 2 * l + 2)
                    V.tensor_scalar(sq[:, h * BANK:(h + 1) * BANK], bank[6 + h][:], EPS, None,
                                    ALU.add).then_inc(var_ready, 1)
                dv.wait_ge(std_ready, l + 1)
                link(V.reciprocal(sq[:, 0:CC * S], sq[:, 0:CC * S]))
                V.tensor_tensor(yf, yf, sq[:, 0:CC * S], ALU.mult).then_inc(yn_ready, 1)
                for n in range(NH):
                    for i in range(NT):
                        dv.wait_ge(wo_psum, 4 * l + 2 * n + i + 1)
                        add_to_x(2 * n + i, i, n).then_inc(x_ready, 1)
                normalise(2 * l + 1)
                if l == 0:
                    for f in range(DFB):
                        dv.wait_ge(dsg_ready, f + 1)
                        if f >= 4:
                            dv.wait_ge(ffn_down, f - 3)
                        V.tensor_tensor(dactT[:, f % 4, :], dsg[:, f % 4, :], bank[4 + f % 4][:, S:2 * S],
                                        ALU.mult).then_inc(dact_ready, 1)
                    dv.wait_ge(dense_psum, 1)
                    for n in range(NH):
                        for i in range(NT):
                            add_to_x(2 * n + i, i, n).then_inc(x_ready, 1)

            def r_(a):
                return rt[:, a]

            def bc(v):
                return v.unsqueeze(2).to_broadcast([P, NT, E])

            dv.wait_ge(logit_psum, 1)
            link(V.tensor_copy(r_(0), bank[0][:, 0:NT * E].rearrange("p (i e) -> p i e", i=NT)))

            def first_max(logit, top, onehot, tmp, idx):
                link(V.tensor_reduce(top, r_(logit), AX_X, ALU.max))
                link(V.tensor_tensor(r_(tmp), r_(logit), bc(top), ALU.is_equal))
                link(V.scalar_tensor_tensor(out=r_(tmp), in0=r_(tmp), scalar=-float(E), in1=eidx[:],
                                            op0=ALU.mult, op1=ALU.add))
                link(V.tensor_reduce(idx, r_(tmp), AX_X, ALU.min))
                link(V.tensor_scalar(idx, idx, float(E), None, ALU.add))
                link(V.tensor_tensor(r_(onehot), eidx[:], bc(idx), ALU.is_equal))

            first_max(0, rv[:, 0, :], 1, 2, rv[:, 4, :])
            link(V.scalar_tensor_tensor(out=r_(3), in0=r_(1), scalar=-3e38, in1=r_(0), op0=ALU.mult, op1=ALU.add))
            first_max(3, rv[:, 1, :], 4, 2, rv[:, 5, :])
            V.tensor_tensor(rv[:, 2, :], rv[:, 1, :], rv[:, 0, :], ALU.subtract).then_inc(lse_ready, 1)
            V.tensor_tensor(r_(5), r_(1), r_(4), ALU.add).then_inc(chosen_ready, 1)
            dv.wait_ge(lexp_ready, 1)
            link(V.tensor_scalar(rv[:, 6, :], rv[:, 3, :], 1.0, None, ALU.add))
            link(V.reciprocal(rv[:, 6, :], rv[:, 6, :]))
            link(V.tensor_tensor(rv[:, 7, :], rv[:, 6, :], rv[:, 3, :], ALU.mult))
            link(V.tensor_tensor(r_(6), r_(1), bc(rv[:, 6, :]), ALU.mult))
            link(V.tensor_tensor(r_(7), r_(4), bc(rv[:, 7, :]), ALU.mult))
            for q in range(PASSES):
                link(V.tensor_tensor(wgt_tab[:, :, q * E:(q + 1) * E], r_(6), r_(7), ALU.add))
            dv.wait_ge(pos_psum, 1)
            link(V.tensor_scalar(r_(8), r_(5), float(4 * S), -float(4 * S), ALU.mult, ALU.add))
            link(V.tensor_tensor(pos_tab[:, :, 0:E], r_(8), bank[1][:, 0:NT * E].rearrange("p (i e) -> p i e", i=NT),
                                 ALU.add))
            for q in range(1, PASSES):
                link(V.tensor_scalar(pos_tab[:, :, q * E:(q + 1) * E], pos_tab[:, :, 0:E], -float(q * CAP), None,
                                     ALU.add))
            link(V.memset(pos_tab[:, :, PASSES * E:], -1.0))
            link(V.tensor_reduce(mcount[:, 0:1], bank[1][:, NT * E:NT * E + E], AX_X, ALU.max))
            link(V.tensor_scalar(mcount[:, 0:1], mcount[:, 0:1], float(CAP), float(E), ALU.is_gt, ALU.mult))
            link(V.tensor_scalar(mcount[:, 0:1], mcount[:, 0:1], float(E), None, ALU.add))
            V.tensor_copy(trips_i[:], mcount[:, 0:1]).then_inc(trips_ready, 1)
            dv.wait_ge(trips_ready, 1)

            def select(j):
                for i in range(NT):
                    last = V.tensor_scalar(sel[:, i, :], iota_f[:], pos_tab[:, i, bass.ds(j, 1)], None, ALU.is_equal)
                    last.then_inc(sel_ready, 1)

            def drain_gather(h, count):
                dv.wait_ge(b7_full, count)
                V.tensor_tensor(xeT[:, 4 * h:4 * h + 4, :], bank[7][:].rearrange("p (k s) -> p k s", k=4),
                                p_(1, "ffn_g", 4 * h, 4).unsqueeze(2).to_broadcast([P, 4, CAP]),
                                ALU.mult).then_inc(b7_drained, 1)

            V.memset(mcount[:, 0:1], 0.0).then_inc(act_ready, 1)
            V.memset(mcount[:, 1:2], 0.0).then_inc(b4_drained, 1)
            select(0)
            drain_gather(0, 1)
            drain_gather(1, 2)
            dv.wait_ge(trips_ready, 1)
            trips = dv.value_load(trips_i[0:1, 0:1], min_val=E, max_val=PASSES * E)
            with dv.Fori(0, trips) as j:
                for i in range(NT):
                    V.tensor_scalar(wsel[:, i, :], iota_f[:], pos_tab[:, i, bass.ds(j, 1)],
                                    wgt_tab[:, i, bass.ds(j, 1)], ALU.is_equal, ALU.mult).then_inc(wsel_ready, 1)
                for c in range(FCH):
                    dv.wait_ge(sg_ready, j * FCH + c + 1)
                    dv.wait_ge(h3_full, j * FCH + c + 1)
                    if c >= 2:
                        dv.wait_ge(b4_full, j * (FCH + 2) + c - 1)
                    V.tensor_tensor(act[:, c % 2, :], sg[:, c % 2, :], bank[2 + c % 2][:],
                                    ALU.mult).then_inc(act_ready, 1)
                    if c == 3:
                        select(j + 1)
                drain_gather(0, j * 5 + 4)
                drain_gather(1, j * 5 + 5)
                for q in range(2 * NT):
                    i, n = divmod(q, 2)
                    if q % 2 == 0:
                        dv.wait_ge(b7_full, j * 5 + 6 + q // 2)
                        add_to_x(7, i, n).then_inc(b7_drained, 1)
                    else:
                        dv.wait_ge(b4_full, j * (FCH + 2) + FCH + 1 + q // 2)
                        add_to_x(4, i, n).then_inc(b4_drained, 1)
            dv.wait_ge(b7_drained, trips * 5 + 2)
            dv.wait_ge(b4_drained, trips * (FCH + 2) + 1)
            V.memset(cmx[:], 0.0).then_inc(trips_done, 1)

        @block.tensor
        def _(pe):
            T = nc.tensor
            pe.wait_ge(const_ready, 7)
            pe.wait_ge(par_loaded, 48)

            def transpose_rows(m):
                for i in range(NT):
                    pe.wait_ge(hn_ready, NT * m + i + 1)
                    for h in range(2):
                        for k in range(4):
                            last = T.transpose(bank[4 + 2 * i + h][:, k * P:(k + 1) * P],
                                               hn[:, i, (4 * h + k) * P:(4 * h + k + 1) * P], ident[:])
                        last.then_inc(hT_psum, 1)
                pe.wait_ge(hT_ready, 4 * (m + 1))

            def product(dst, lhs, rhs, chunks):
                for n, k in enumerate(chunks):
                    last = T.matmul(dst, lhs(k), rhs(k), start=(n == 0), stop=(n == len(chunks) - 1))
                return last

            for l in range(L):
                transpose_rows(2 * l)
                wait_static(pe, "win", l, 0)
                wait_static(pe, "win", l, 1)
                for c in range(CC):
                    if c >= 2:
                        pe.wait_ge(u_ready, CC * l + c - 1)
                    for half in range(2):
                        w = view("win", l, half)
                        last = product(bank[c % 2][:, half * S:(half + 1) * S],
                                       lambda k: w[:, k, c * P:(c + 1) * P], lambda k: hT[:, k, :], range(KD))
                    last.then_inc(glu_psum, 1)
                for n in range(6):
                    c, i = divmod(n, NT)
                    if i == 0:
                        wait_static(pe, "win", l, 2 + c)
                    w = view("win", l, 2 + c)
                    product(bank[2 + n][:, 0:w.shape[2]], lambda k: hT[:, k, i * P:(i + 1) * P],
                            lambda k: w[:, k, :], range(KD)).then_inc(z_psum, 1)
                pe.wait_ge(zdup_ready, NT * (l + 1))
                for a in range(2):
                    for kv in range(KV):
                        for i in range(NT):
                            last = T.transpose(bank[3 + a][:, kv * S + i * P:kv * S + (i + 1) * P],
                                               zdup[:, i, 2 * a + kv].rearrange("p e d -> p (e d)"), ident[:])
                    last.then_inc(zdup_psum, 1)
                pe.wait_ge(qkn_ready, 8 * (l + 1))
                for i in range(NT):
                    for g in range(G):
                        last = T.transpose(bank[i][:, g * P:(g + 1) * P],
                                           qn[:, i, g].rearrange("p k d -> p (k d)"), ident[:])
                    last.then_inc(qkT_psum, 1)
                for b in range(2):
                    for i in range(NT):
                        last = T.transpose(bank[2][:, b * S + i * P:b * S + (i + 1) * P],
                                           kn[:, i, b].rearrange("p k d -> p (k d)"), ident[:])
                last.then_inc(qkT_psum, 1)
                r0 = 32 * l
                for a in range(2):
                    wait_static(pe, "cmp", l, a)
                    pe.wait_ge(blk_ready, 16 * l + 8 * (a + 1))
                    w = view("cmp", l, a)
                    for k in range(LP):
                        T.matmul(bank[5 + a][0:MC, 0:HID], blkT[:, a, k, 0:MC], w[:, k, :], start=(k == 0), stop=False)
                    T.matmul(bank[5 + a][0:MC, 0:HID], ones[r0:r0 + 1, 0:MC], rows_sb[r0:r0 + 1, a * HID:(a + 1) * HID],
                             start=False, stop=True).then_inc(hid_psum, 1)
                pe.wait_ge(hid_ready, 2 * (l + 1))
                for a in range(2):
                    for k in range(2):
                        q = 2 * a + k
                        last = T.transpose(bank[7][:, q * 2 * CPAD:q * 2 * CPAD + MC],
                                           hid[0:MC, a, k * P:(k + 1) * P], ident[0:MC, 0:MC])
                last.then_inc(hidT_psum, 1)
                pe.wait_ge(hidT_ready, l + 1)
                for a in range(2):
                    for k in range(2):
                        w2 = par[:, l, col["w2"] + (2 * a + k) * HD:col["w2"] + (2 * a + k + 1) * HD]
                        T.matmul(bank[5 + a][0:MC, 0:HD], hidT[:, 2 * a + k, 0:MC], w2, start=(k == 0), stop=False)
                    T.matmul(bank[5 + a][0:MC, 0:HD], ones[r0:r0 + 1, 0:MC],
                             rows_sb[r0:r0 + 1, 2 * HID + a * HD:2 * HID + (a + 1) * HD],
                             start=False, stop=True).then_inc(cmp_psum, 1)
                pe.wait_ge(kcn_ready, l + 1)
                T.transpose(bank[7][:, 0:MC], kcn[0:MC].rearrange("p e d -> p (e d)"),
                            ident[0:MC, 0:MC]).then_inc(kcT_psum, 1)
                pe.wait_ge(qkT_ready, 4 * (l + 1))
                pe.wait_ge(kcT_ready, l + 1)
                pe.wait_ge(vc_ready, l + 1)
                for kv in range(KV):
                    r = slice(kv * HD, (kv + 1) * HD)
                    for i in range(NT):
                        for g in range(G):
                            o = (i * G + g) * CPAD
                            last = T.matmul(bank[6 + kv][:, o:o + NCMP], qT[r, g, i * P:(i + 1) * P],
                                            kcT[r, kv * CPAD:kv * CPAD + NCMP], start=True, stop=True)
                    last.then_inc(cs_psum, 1)

                def score(n):
                    gi, kv, i, b, h0, nh = units[n]
                    keys = (i + 1) * P
                    if n >= 2:
                        pe.wait_ge(s_ready, NU * l + n - 1)
                    r = slice(kv * HD, (kv + 1) * HD)
                    for h in range(nh):
                        last = T.matmul(bank[n % 2][:, h * keys:(h + 1) * keys], qT[r, h0 + h, i * P:(i + 1) * P],
                                        kT[r, b, 0:keys], start=True, stop=True)
                    last.then_inc(s_psum, 1)

                def transpose_probs(n):
                    gi, kv, i, b, h0, nh = units[n]
                    keys = (i + 1) * P
                    pe.wait_ge(p_ready, NU * l + n + 1)
                    if n >= 2:
                        pe.wait_ge(pT_ready, NU * l + n - 1)
                    for k in range(i + 1):
                        for h in range(nh):
                            last = T.transpose(bank[2 + n % 2][:, (k * nh + h) * P:(k * nh + h + 1) * P],
                                               probs[:, n % 2, h * keys + k * P:h * keys + (k + 1) * P], ident[:])
                    last.then_inc(pT_psum, 1)

                def values(gi):
                    kv, i = groups[gi]
                    r = slice(kv * HD, (kv + 1) * HD)
                    c = slice(kv * CPAD, kv * CPAD + NCMP)
                    pe.wait_ge(pT_ready, NU * l + group_last[gi] + 1)
                    dst = bank[4 + i][r, :]
                    T.matmul(dst, vc[c, :], cpT[c, i, :], start=True, stop=False)
                    for b in range(2):
                        for k in range(i + 1):
                            v0 = (VS0, VW0)[b] + kv * HD
                            last = T.matmul(dst, z[:, k, v0:v0 + HD], probsT[:, gi % 2, b, k, :],
                                            start=False, stop=(b == 1 and k == i))
                    last.then_inc(o_psum, 1)

                score(0)
                score(1)
                pe.wait_ge(cp_ready, l + 1)
                for i in range(NT):
                    for g in range(G):
                        last = T.transpose(bank[6 + i][0:2 * CPAD, g * P:(g + 1) * P],
                                           cp[:, i, g].rearrange("p k c -> p (k c)"), ident[:])
                last.then_inc(cpT_psum, 1)
                pe.wait_ge(cpT_ready, NT * (l + 1))
                for n in range(NU):
                    transpose_probs(n)
                    if n + 2 < NU:
                        score(n + 2)
                    for gi in range(len(groups)):
                        if n == group_last[gi] + 1:
                            values(gi)
                values(len(groups) - 1)
                pe.wait_ge(conv_step, CC * TAPS * (l + 1))
                for h in range(2):
                    T.matmul(bank[6 + h][:], group_mean[:], y[:, 2 * h:2 * h + 2, :].rearrange("p c t -> p (c t)"),
                             start=True, stop=True).then_inc(mean_psum, 1)
                pe.wait_ge(centred_ready, 3 * (l + 1))
                for h in range(2):
                    T.matmul(bank[6 + h][:], group_mean[:], sq[:, h * BANK:(h + 1) * BANK],
                             start=True, stop=True).then_inc(var_psum, 1)
                pe.wait_ge(mix_ready, 4 * (l + 1))
                pe.wait_ge(conv_mix, CC * (l + 1))
                for n in range(NH):
                    wait_static(pe, "wout", l, n)
                    w = view("wout", l, n)
                    for i in range(NT):
                        product(bank[2 * n + i][:], lambda k: mixT[:, k, i * P:(i + 1) * P], lambda k: w[:, k, :],
                                range(KD)).then_inc(wo_psum, 1)
                transpose_rows(2 * l + 1)
                if l == 0:
                    def up(f):
                        c, j = divmod(f, FB)
                        if j == 0:
                            wait_static(pe, "d1", l, c)
                            wait_static(pe, "d3", l, c)
                        if f >= 4:
                            pe.wait_ge(dact_ready, f - 3)
                        for half, kind in enumerate(("d1", "d3")):
                            w = view(kind, l, c)
                            last = product(bank[4 + f % 4][:, half * S:(half + 1) * S],
                                           lambda k: w[:, k, j * P:(j + 1) * P], lambda k: hT[:, k, :], range(KD))
                        last.then_inc(ffn_psum, 1)

                    def down(f):
                        c, j = divmod(f, FB)
                        if j == 0:
                            wait_static(pe, "d2", l, c)
                        pe.wait_ge(dact_ready, f + 1)
                        w = view("d2", l, c)
                        for n in range(NH):
                            for i in range(NT):
                                last = T.matmul(bank[2 * n + i][:], dactT[:, f % 4, i * P:(i + 1) * P],
                                                w[:, j, n * BANK:(n + 1) * BANK], start=(f == 0), stop=(f == DFB - 1))
                        last.then_inc(ffn_down, 1)

                    up(0)
                    for f in range(1, DFB):
                        up(f)
                        down(f - 1)
                    down(DFB - 1)
                    pe.wait_ge(ffn_down, DFB)
                    T.transpose(bank[7][:, 0:P], ident[:], ident[:]).then_inc(dense_psum, 1)

            for i in range(NT):
                last = product(bank[0][:, i * E:(i + 1) * E], lambda k: hT[:, k, i * P:(i + 1) * P],
                               lambda k: router_sb[:, k, :], range(KD))
            last.then_inc(logit_psum, 1)
            pe.wait_ge(chosen_ready, 1)
            chosen = rt[:, 5]
            T.matmul(bank[1][:, 0:E], before[:], chosen[:, 0, :], start=True, stop=True)
            T.matmul(bank[1][:, E:2 * E], ones[:], chosen[:, 0, :], start=True, stop=False)
            T.matmul(bank[1][:, E:2 * E], before[:], chosen[:, 1, :], start=False, stop=True)
            T.matmul(bank[1][:, 2 * E:3 * E], ones[:], chosen[:, 0, :], start=True, stop=False)
            T.matmul(bank[1][:, 2 * E:3 * E], ones[:], chosen[:, 1, :], start=False, stop=True).then_inc(pos_psum, 1)

            def gather(h):
                for k in range(4):
                    kk = 4 * h + k
                    for i in range(NT):
                        last = T.matmul(bank[7][:, k * CAP:(k + 1) * CAP], hn[:, i, kk * P:(kk + 1) * P],
                                        sel[:, i, :], start=(i == 0), stop=(i == NT - 1))
                last.then_inc(b7_full, 1)

            pe.wait_ge(sel_ready, NT)
            gather(0)
            pe.wait_ge(b7_drained, 1)
            gather(1)
            pe.wait_ge(trips_ready, 1)
            trips = pe.value_load(trips_i[0:1, 0:1], min_val=E, max_val=PASSES * E)
            with pe.Fori(0, trips) as j:
                def up(c):
                    pe.wait_ge(act_ready, j * FCH + max(c - 1, 0) + 1)
                    for kind, b, full in (("e1", c % 2, h1_full), ("e3", 2 + c % 2, h3_full)):
                        wait_expert(pe, kind, c, j)
                        w = expert_view(kind, c)
                        product(bank[b][:], lambda k: xeT[:, k, :], lambda k: w[:, k, :], range(KD)).then_inc(full, 1)

                def down(c):
                    pe.wait_ge(act_ready, j * FCH + c + 2)
                    pe.wait_ge(b4_drained, j * (FCH + 2) + c + 1)
                    for k in range(FB):
                        last = T.transpose(bank[4][:, k * P:(k + 1) * P], act[:, c % 2, k * P:(k + 1) * P], ident[:])
                    last.then_inc(b4_full, 1)
                    if c == 0:
                        pe.wait_ge(y_drained, j * NH + 1)
                    wait_expert(pe, "e2", c, j)
                    pe.wait_ge(b4_drained, j * (FCH + 2) + c + 2)
                    w = expert_view("e2", c)
                    for k in range(FB):
                        for n in range(NH):
                            last = T.matmul(bank[5 + n][:], actT[:, c % 2, k * P:(k + 1) * P],
                                            w[:, k, n * BANK:(n + 1) * BANK],
                                            start=(c == 0 and k == 0), stop=(c == FCH - 1 and k == FB - 1))
                    last.then_inc(down_done, 1)

                pe.wait_ge(b7_drained, j * 5 + 2)
                up(0)
                for c in range(1, FCH):
                    up(c)
                    if c == FCH - 1:
                        pe.wait_ge(sel_ready, (j + 2) * NT)
                        pe.wait_ge(b7_drained, j * 5 + 3)
                        gather(0)
                    down(c - 1)
                    if c == 2:
                        pe.wait_ge(wsel_ready, (j + 1) * NT)
                        for i in range(NT):
                            last = T.transpose(bank[7][:, i * P:(i + 1) * P], wsel[:, i, :], ident[:])
                        last.then_inc(b7_full, 1)
                pe.wait_ge(b7_drained, j * 5 + 4)
                gather(1)
                down(FCH - 1)
                pe.wait_ge(y_drained, (j + 1) * NH + 1)
                pe.wait_ge(b7_drained, j * 5 + 5)
                for q in range(2 * NT):
                    i, n = divmod(q, 2)
                    b, full = ((7, b7_full), (4, b4_full))[q % 2]
                    if q == 1:
                        pe.wait_ge(b4_drained, j * (FCH + 2) + FCH + 1)
                    if q == 2:
                        pe.wait_ge(b7_drained, j * 5 + 6)
                    if q == 3:
                        pe.wait_ge(b4_drained, j * (FCH + 2) + FCH + 2)
                    T.matmul(bank[b][:], wselT[:, i * P:(i + 1) * P], ye[:, n * BANK:(n + 1) * BANK],
                             start=True, stop=True).then_inc(full, 1)


def kernel(**inputs):
    import numpy as np
    import concourse.bacc as bacc
    from concourse import mybir as mb
    from concourse.bass_utils import run_bass_kernel_spmd

    a = {name: np.asarray(v) for name, v in inputs.items()}
    B, S, D = a["x"].shape
    L, P = a["w_in"].shape[0], 128
    HD, KV, G = 64, 2, 4

    def cols(v):
        return v.reshape(L, -1, P).transpose(0, 2, 1)

    def both(v):
        return np.concatenate([v, v], axis=2).transpose(0, 2, 1)

    def positions(v):
        return v.reshape(L, -1, 2, HD).transpose(0, 2, 3, 1).reshape(L, P, -1)

    def second(v):
        return v.reshape(L, -1, P, HD).transpose(0, 2, 1, 3).reshape(L, P, -1)

    taps = a["conv_dw_w"].transpose(0, 2, 1)
    small = np.concatenate([
        cols(a["attn_norm_g"]), cols(a["ffn_norm_g"]),
        taps.reshape(L, -1, P, taps.shape[2]).transpose(0, 2, 1, 3).reshape(L, P, -1),
        cols(a["conv_dw_b"]), cols(a["conv_ln_g"]), cols(a["conv_ln_b"]),
        both(a["q_norm_g"][:, None, :]), both(a["k_norm_g"]),
        positions(a["cmp_pos_k"]), positions(a["cmp_pos_v"]),
        second(a["cmp_k_w2"]), second(a["cmp_v_w2"])], axis=2)
    rows = np.concatenate([a["cmp_k_b1"], a["cmp_v_b1"], a["cmp_k_b2"], a["cmp_v_b2"]], axis=1)
    wo = a["w_out"]
    half = wo.shape[1] // 2
    att = wo[:, half:].reshape(L, KV, G, HD, D).transpose(0, 2, 1, 3, 4).reshape(L, half, D)
    w_out = np.concatenate([wo[:, :half], att], axis=1)

    args = [("x", a["x"][0]), ("w_in", a["w_in"]), ("cmp_k_w1", a["cmp_k_w1"]), ("cmp_v_w1", a["cmp_v_w1"]),
            ("w_out", w_out), ("dense_w1", a["dense_w1"][0]), ("dense_w3", a["dense_w3"][0]),
            ("dense_w2", a["dense_w2"][0]), ("moe_w1", a["moe_w1"][0]), ("moe_w3", a["moe_w3"][0]),
            ("moe_w2", a["moe_w2"][0]), ("small", small), ("rows", rows), ("router", a["router_w"][0])]
    nc = bacc.Bacc("TRN2", target_bir_lowering=False, num_devices=1)
    arrays, aps = {}, []
    for name, v in args:
        v = np.ascontiguousarray(v)
        arrays["in_" + name] = v
        aps.append(nc.dram_tensor("in_" + name, v.shape, mb.dt.from_np(v.dtype), kind="ExternalInput").ap())
    out = nc.dram_tensor("out_0", (S, D), mb.dt.float32, kind="ExternalOutput").ap()
    hymba_trunk(nc, *aps, out)
    r = run_bass_kernel_spmd(nc, [arrays], core_ids=[0])
    return r.results[0]["out_0"].reshape(B, S, D)
```

```python
from contextlib import ExitStack

import concourse.bass as bass
from concourse import mybir

P = 128
BANK = 512
ALU = mybir.AluOpType
ACT = mybir.ActivationFunctionType
F32 = mybir.dt.float32
F32R = mybir.dt.float32r
I32 = mybir.dt.int32
AX_X = mybir.AxisListType.X
NEG = -1e30
EPS = 1e-6


def hymba_trunk(nc, x, w_in, cmp_k_w1, cmp_v_w1, w_out, dense_w1, dense_w3, dense_w2,
                moe_w1, moe_w3, moe_w2, small, rows, router, out):
    S, D = x.shape
    L = w_in.shape[0]
    CONV = w_out.shape[1] // 2
    HD, KV, G = 64, 2, 4
    H = KV * G
    TAPS = 31
    CMP_BLOCK, CMP_STRIDE = 32, 16
    NCMP = (S - CMP_BLOCK) // CMP_STRIDE + 1
    CPAD = 32
    MC = CPAD + NCMP
    HID = cmp_k_w1.shape[2]
    FD = dense_w1.shape[1]
    E, FE = moe_w1.shape[0], moe_w1.shape[2]
    NT = S // P
    KD = D // P
    NH = D // BANK
    CC = CONV // P
    LP = CMP_BLOCK * HD // P
    ZA = w_in.shape[2] - 2 * CONV
    AW = H * HD
    KC0, VC0, KS0, VS0, KW0, VW0, GL0 = [AW + i * KV * HD for i in range(7)]
    PAD = TAPS - 1
    CAP = P
    PASSES = S // CAP
    FCH = FE // BANK
    FB = BANK // P
    assert NT == 2 and NH == 2 and S <= 512 and FE % BANK == 0 and FD % P == 0 and L == 2

    sizes = [("attn_g", KD), ("ffn_g", KD), ("conv_w", CC * TAPS), ("conv_b", CC), ("ln_g", CC), ("ln_b", CC),
             ("q_g", 1), ("k_g", 3), ("pos", 2 * LP), ("w2", 2 * (HID // P) * HD)]
    col, at = {}, 0
    for name, n in sizes:
        col[name] = at
        at += n
    NSM = at
    assert small.shape[2] == NSM

    SLOTS, SLOT, PIECE, RAW, SPLIT = 4, 8 * BANK, 4 * BANK, 7, 3
    DG = 2 * P
    NDG = FD // DG
    assert FD % DG == 0
    stream = []
    for l in range(L):
        stream += [("win", l, c) for c in range(5)] + [("cmp", l, 0), ("cmp", l, 1)]
        stream += [("wout", l, 0), ("wout", l, 1)]
        if l == 0:
            stream += [("d1", 0, 0), ("d3", 0, 0)]
            for g in range(1, NDG):
                stream += [("d1", 0, g), ("d3", 0, g), ("d2", 0, g - 1)]
            stream += [("d2", 0, NDG - 1)]
    slots = [key for key in stream if key[0][0] != "d"]
    pieces = [key for key in stream if key[0][0] == "d"]
    slot_of = {key: n for n, key in enumerate(slots)}
    piece_of = {key: n for n, key in enumerate(pieces)}
    BASE = len(pieces)
    expert_stream = [("e1", 0, 0), ("e1", 0, 1), ("e3", 0, 0), ("e3", 0, 1)]
    for c in range(1, FCH):
        expert_stream += [("e1", c, 0), ("e1", c, 1), ("e3", c, 0), ("e3", c, 1), ("e2", c - 1, 0), ("e2", c - 1, 1)]
    expert_stream += [("e2", FCH - 1, 0), ("e2", FCH - 1, 1)]
    XS = len(expert_stream)
    xplace = {key: m for m, key in enumerate(expert_stream)}
    assert XS % RAW == 0 and XS % SPLIT == 0 and BASE % SPLIT == 0

    ctx = ExitStack()
    with ctx:
        def sb(name, shape, dt=F32):
            return ctx.enter_context(nc.sbuf_tensor(name, shape, dt))

        def sem(name):
            return ctx.enter_context(nc.semaphore(name))

        ring = sb("ring", [P, SLOTS * SLOT])
        w_hi = [sb(f"w_hi{n}", [P, PIECE], F32R) for n in range(SPLIT)]
        w_lo = [sb(f"w_lo{n}", [P, PIECE], F32R) for n in range(SPLIT)]
        x_sb = sb("x_sb", [P, NT, D])
        hn = sb("hn", [P, NT, D])
        hT = sb("hT", [P, KD, S])
        mixT = sb("mixT", [P, KD, S])
        par = sb("par", [P, L, NSM])
        rows_sb = sb("rows_sb", [33, rows.shape[1]])
        router_sb = sb("router_sb", [P, KD, E])
        ident = sb("ident", [P, P])
        before = sb("before", [P, P])
        ones = sb("ones", [P, P])
        group_mean = sb("group_mean", [P, P])
        iota_f = sb("iota_f", [P, P])
        causal = sb("causal", [P, 2 * P])
        cmask = sb("cmask", [P, NT, NCMP])
        cneg = sb("cneg", [P, NT, NCMP])
        minus_half = sb("minus_half", [P, 24])
        ss = sb("ss", [P, 2])
        rms = sb("rms", [P, 2])
        stat = sb("stat", [P, 24])
        rstat = sb("rstat", [P, 24])
        cstat = sb("cstat", [P, 2])
        gates = sb("gates", [P, NT, 24])
        negmax = sb("negmax", [P, 2, G])
        psumr = sb("psumr", [P, 2, G])
        pscale = sb("pscale", [P, 2, G])
        cmx = sb("cmx", [P, NT * H])
        csum = sb("csum", [P, NT * H])
        crs = sb("crs", [P, NT * H])
        rt = sb("rt", [P, 16, NT, E])
        rv = sb("rv", [P, 8, NT])
        eidx = sb("eidx", [P, NT, E])
        pos_tab = sb("pos_tab", [P, NT, PASSES * E + 1])
        wgt_tab = sb("wgt_tab", [P, NT, PASSES * E + 1])
        mcount = sb("mcount", [P, 2])
        trips_i = sb("trips_i", [P, 1], I32)

        cp = sb("cp", [P, NT, G, KV, CPAD])
        kcn = sb("kcn", [P, 2, HD])
        kcT = sb("kcT", [P, MC])
        vc = sb("vc", [P, HD])

        attention_phase, dense_phase, expert_phase = ExitStack(), ExitStack(), ExitStack()

        ARENA = 11944
        arena = attention_phase.enter_context(nc.sbuf_tensor("arena", [P, ARENA], F32))

        def carve(sizes):
            at, got = 0, []
            for n in sizes:
                got.append(arena[:, at:at + n])
                at += n
            assert at <= ARENA, at
            return got

        z_, qT_, kT_, pt_, u_, y_, sq_, sig_ = carve(
            [NT * ZA, G * S, 2 * S, 2 * 4 * BANK, CC * (PAD + S), CC * S, 2 * BANK, 2 * S])
        z = z_.rearrange("p (i c) -> p i c", i=NT)
        qT = qT_.rearrange("p (g t) -> p g t", g=G)
        kT = kT_.rearrange("p (b t) -> p b t", b=2)
        probsT = pt_.rearrange("p (w b k n) -> p w b k n", w=2, b=2, k=2)
        u = u_.rearrange("p (c t) -> p c t", c=CC)
        y = y_.rearrange("p (c t) -> p c t", c=CC)
        sq = sq_
        sig = sig_.rearrange("p (b t) -> p b t", b=2)
        zdup = pt_[:, 0:NT * 4 * P].rearrange("p (i a e d) -> p i a e d", i=NT, a=4, e=2)
        hid = pt_[:, 1024:1024 + 2 * HID].rearrange("p (a n) -> p a n", a=2)
        hidT = pt_[:, 1536:1536 + 4 * CPAD * 2].rearrange("p (a n) -> p a n", a=4)
        blkT = pt_[:, 2048:2048 + 2 * LP * 2 * CPAD].rearrange("p (a l m) -> p a l m", a=2, l=LP)
        hn_flat = hn[:].rearrange("p i d -> p (i d)")
        qn = hn_flat[:, 0:NT * AW].rearrange("p (i g k d) -> p i g k d", i=NT, g=G, k=KV)
        kn = hn_flat[:, NT * AW:NT * AW + NT * 2 * P].rearrange("p (i b k d) -> p i b k d", i=NT, b=2, k=KV)
        scores = hn_flat[:, 0:2 * BANK].rearrange("p (a n) -> p a n", a=2)
        probs = hn_flat[:, 2 * BANK:4 * BANK].rearrange("p (a n) -> p a n", a=2)
        cpT = sq_[:, 0:NT * BANK].rearrange("p (i n) -> p i n", i=NT)
        attention_phase.close()

        def sb_d(name, shape, dt=F32):
            return dense_phase.enter_context(nc.sbuf_tensor(name, shape, dt))

        hT_hi, hT_lo = sb_d("hT_hi", [P, KD, S], F32R), sb_d("hT_lo", [P, KD, S], F32R)
        dact_hi, dact_lo = sb_d("dact_hi", [P, 2, S], F32R), sb_d("dact_lo", [P, 2, S], F32R)
        dsg, dact = sb_d("dsg", [P, 2, 2 * S]), sb_d("dact", [P, 2, 2 * S])
        dense_phase.close()

        def sb_e(name, shape, dt=F32):
            return expert_phase.enter_context(nc.sbuf_tensor(name, shape, dt))

        h_hi, h_lo = sb_e("h_hi", [P, NT, D], F32R), sb_e("h_lo", [P, NT, D], F32R)
        xe_hi, xe_lo = sb_e("xe_hi", [P, KD, CAP], F32R), sb_e("xe_lo", [P, KD, CAP], F32R)
        actT_hi, actT_lo = sb_e("actT_hi", [P, BANK], F32R), sb_e("actT_lo", [P, BANK], F32R)
        ye_hi, ye_lo = sb_e("ye_hi", [P, D], F32R), sb_e("ye_lo", [P, D], F32R)
        sel = sb_e("sel", [P, NT, CAP], F32R)
        selT = sb_e("selT", [P, S], F32R)
        sel_f = sb_e("sel_f", [P, NT, CAP])
        slot_weight = sb_e("slot_weight", [P, 1])
        sg = hn_flat[:, 0:2 * BANK].rearrange("p (a n) -> p a n", a=2)
        act = hn_flat[:, 2 * BANK:4 * BANK].rearrange("p (a n) -> p a n", a=2)
        expert_phase.close()

        bank = [ctx.enter_context(nc.psum_tensor(f"bank{b}", [P, BANK], F32)) for b in range(8)]

        x_loaded, par_loaded = sem("x_loaded"), sem("par_loaded")
        slot_arrived = [sem(f"slot{s}_arrived") for s in range(SLOTS)]
        piece_arrived = [sem(f"piece{s}_arrived") for s in range(RAW)]
        const_step, const_ready = sem("const_step"), sem("const_ready")
        pads_ready = sem("pads_ready")
        ss_ready, ms_ready, rms_ready, hn_ready = sem("ss_ready"), sem("ms_ready"), sem("rms_ready"), sem("hn_ready")
        hT_psum, hT_ready = sem("hT_psum"), sem("hT_ready")
        glu_psum, sig_ready, u_ready, conv_step = sem("glu_psum"), sem("sig_ready"), sem("u_ready"), sem("conv_step")
        conv_done = sem("conv_done")
        z_psum, z_ready = sem("z_psum"), sem("z_ready")
        zdup_ready, zdup_psum, blk_ready = sem("zdup_ready"), sem("zdup_psum"), sem("blk_ready")
        hid_psum, hid_ready, hidT_psum, hidT_ready = sem("hid_psum"), sem("hid_ready"), sem("hidT_psum"), sem("hidT_ready")
        cmp_psum, vc_ready, kcn_ready, kcT_psum, kcT_ready = (
            sem("cmp_psum"), sem("vc_ready"), sem("kcn_ready"), sem("kcT_psum"), sem("kcT_ready"))
        stat_ready, rstat_ready, cstat_ready, rcstat_ready = (
            sem("stat_ready"), sem("rstat_ready"), sem("cstat_ready"), sem("rcstat_ready"))
        qkn_ready, qkT_psum, qkT_ready = sem("qkn_ready"), sem("qkT_psum"), sem("qkT_ready")
        cs_psum, cs_ready, cexp_ready, cp_ready, cpT_psum, cpT_ready = (
            sem("cs_psum"), sem("cs_ready"), sem("cexp_ready"), sem("cp_ready"), sem("cpT_psum"), sem("cpT_ready"))
        gates_ready = sem("gates_ready")
        s_psum, s_ready, exp_ready, p_ready, pT_psum, pT_ready = (
            sem("s_psum"), sem("s_ready"), sem("exp_ready"), sem("p_ready"), sem("pT_psum"), sem("pT_ready"))
        o_psum, mix_ready = sem("o_psum"), sem("mix_ready")
        squares_ready = sem("squares_ready")
        mean_psum, centred_ready, var_psum, rvar_ready, std_ready, yn_ready, conv_mix = (
            sem("mean_psum"), sem("centred_ready"), sem("var_psum"), sem("rvar_ready"), sem("std_ready"),
            sem("yn_ready"), sem("conv_mix"))
        wo_psum, x_ready = sem("wo_psum"), sem("x_ready")
        w_hi_ready, w_lo_ready, w_used = sem("w_hi_ready"), sem("w_lo_ready"), sem("w_used")
        hTs_hi, hTs_ready = sem("hTs_hi"), sem("hTs_ready")
        dsg_ready, dact_ready, dact_hi_ready, dact_lo_ready = (
            sem("dsg_ready"), sem("dact_ready"), sem("dact_hi_ready"), sem("dact_lo_ready"))
        dve_step, act_step = sem("dve_step"), sem("act_step")
        logit_psum, lse_ready, lexp_ready, chosen_ready, pos_psum, trips_ready = (
            sem("logit_psum"), sem("lse_ready"), sem("lexp_ready"), sem("chosen_ready"), sem("pos_psum"),
            sem("trips_ready"))
        hback_psum, h_hi_ready, h_split = sem("hback_psum"), sem("h_hi_ready"), sem("h_split")
        sg_ready, act_ready = sem("sg_ready"), sem("act_ready")
        actT_psum, actT_hi_ready, actT_ready = sem("actT_psum"), sem("actT_hi_ready"), sem("actT_ready")
        sel_ready, self_ready, selT_psum, selT_ready = (
            sem("sel_ready"), sem("self_ready"), sem("selT_psum"), sem("selT_ready"))
        xe_psum, xe_hi_ready, xe_lo_ready = sem("xe_psum"), sem("xe_hi_ready"), sem("xe_lo_ready")
        ye_hi_ready, ye_lo_ready, back_psum, added = (
            sem("ye_hi_ready"), sem("ye_lo_ready"), sem("back_psum"), sem("added"))
        trips_done, stored = sem("trips_done"), sem("stored")

        def slot(n):
            return ring[:, (n % SLOTS) * SLOT:(n % SLOTS + 1) * SLOT]

        def raw(t):
            return ring[:, (t % RAW) * PIECE:(t % RAW + 1) * PIECE]

        def source(kind, l, c):
            if kind == "win":
                n = min(BANK, w_in.shape[2] - c * BANK)
                return w_in[l, :, c * BANK:c * BANK + n].rearrange("(k p) n -> p k n", p=P), KD, n
            if kind == "cmp":
                w = (cmp_k_w1, cmp_v_w1)[c]
                return w[l].rearrange("(k p) n -> p k n", p=P), LP, HID
            if kind == "wout":
                return w_out[l, :, c * BANK:(c + 1) * BANK].rearrange("(k p) n -> p k n", p=P), KD, BANK
            if kind == "d2":
                return dense_w2[c * DG:(c + 1) * DG, :].rearrange("(k p) n -> p k n", p=P), DG // P, D
            w = dense_w1 if kind == "d1" else dense_w3
            return w[:, c * DG:(c + 1) * DG].rearrange("(k p) n -> p k n", p=P), KD, DG

        def view(kind, l, c):
            _, k, n = source(kind, l, c)
            return slot(slot_of[kind, l, c])[:, 0:k * n].rearrange("p (k n) -> p k n", k=k)

        def split_views(t, k):
            return [w[t % SPLIT][:].rearrange("p (k n) -> p k n", k=k) for w in (w_hi, w_lo)]

        def last_read(key):
            kind, l, c = key
            if kind[0] == "d":
                return w_lo_ready, piece_of[key] + 1
            return {"win": (glu_psum, CC * (l + 1)) if c < 2 else (z_psum, 6 * l + 2 * (c - 1)),
                    "cmp": (hid_psum, 2 * l + c + 1),
                    "wout": (wo_psum, 2 * NT * l + NH * (NT - 1) + c + 1)}[kind]

        def wait_slot(eng, kind, l, c):
            n = slot_of[kind, l, c]
            eng.wait_ge(slot_arrived[n % SLOTS], 16 * (n // SLOTS + 1))

        def wait_raw(eng, t, j=0):
            eng.wait_ge(piece_arrived[t % RAW], 16 * (t // RAW + 1) + j * (16 * XS // RAW))

        units = []
        groups = [(kv, i) for i in range(NT) for kv in range(KV)]
        for gi, (kv, i) in enumerate(groups):
            for b in range(2):
                for h0 in range(0, G, G // (i + 1)):
                    units.append((gi, kv, i, b, h0, G // (i + 1)))
        NU = len(units)
        group_last = [max(n for n, un in enumerate(units) if un[0] == gi) for gi in range(len(groups))]

        def exp_count(l, n):
            return l * sum(un[5] for un in units) + sum(un[5] for un in units[:n + 1])

        BACK = (1, 3, 7, 4)

        block = ctx.enter_context(nc.Block())

        @block.sync
        def _(sp):
            for i in range(NT):
                sp.dma_start(x_sb[:, i, :], x[i * P:(i + 1) * P, :]).then_inc(x_loaded, 16)
            tenant = {}
            for key in stream:
                if key in slot_of:
                    n = slot_of[key]
                    parts, dst, arrived = (2 * (n % SLOTS), 2 * (n % SLOTS) + 1), slot(n), slot_arrived[n % SLOTS]
                else:
                    t = piece_of[key]
                    parts, dst, arrived = (t % RAW,), raw(t), piece_arrived[t % RAW]
                for before_it in dict.fromkeys(tenant[q] for q in parts if q in tenant):
                    sp.wait_ge(*last_read(before_it))
                tenant.update({q: key for q in parts})
                src, k, m = source(*key)
                sp.dma_start(dst[:, 0:k * m].rearrange("p (k n) -> p k n", k=k), src).then_inc(arrived, 16)

            def stream_expert(j, e, first):
                w1 = moe_w1[e].rearrange("(k p) n -> p k n", p=P)
                w3 = moe_w3[e].rearrange("(k p) n -> p k n", p=P)
                w2 = moe_w2[e].rearrange("(k p) n -> p k n", p=P)
                for m, (kind, c, half) in enumerate(expert_stream):
                    t = BASE + m
                    if first and m < RAW:
                        for before_it in dict.fromkeys([tenant[t % RAW]]):
                            sp.wait_ge(*last_read(before_it))
                    else:
                        sp.wait_ge(w_lo_ready, j * XS + (t - RAW + 1))
                    if kind == "e2":
                        src = w2[:, c * FB + 2 * half:c * FB + 2 * half + 2, :]
                        dst = raw(t).rearrange("p (k n) -> p k n", k=2)
                    else:
                        src = (w1 if kind == "e1" else w3)[:, 4 * half:4 * half + 4, c * BANK:(c + 1) * BANK]
                        dst = raw(t).rearrange("p (k n) -> p k n", k=4)
                    sp.dma_start(dst, src).then_inc(piece_arrived[t % RAW], 16)

            stream_expert(0, 0, True)
            with sp.Fori(1, E) as j:
                stream_expert(j, j, False)
            sp.wait_ge(trips_ready, 1)
            trips = sp.value_load(trips_i[0:1, 0:1], min_val=E, max_val=PASSES * E)
            with sp.If(trips > E):
                with sp.Fori(E, PASSES * E) as j:
                    stream_expert(j, j - E, False)
            sp.wait_ge(trips_done, 1)
            for i in range(NT):
                sp.dma_start(out[i * P:(i + 1) * P, :], x_sb[:, i, :]).then_inc(stored, 16)
            sp.wait_ge(stored, 16 * NT)

        @block.gpsimd
        def _(pl):
            nc.gpsimd.memset(ident[:], 0.0).then_inc(const_step, 1)
            nc.gpsimd.memset(ones[:], 1.0).then_inc(const_step, 1)
            nc.gpsimd.memset(causal[:], 0.0).then_inc(const_step, 1)
            nc.gpsimd.memset(cmask[:], 1.0).then_inc(const_step, 1)
            nc.gpsimd.memset(cneg[:], 0.0).then_inc(const_step, 1)
            nc.gpsimd.memset(group_mean[:], 1.0 / HD).then_inc(const_step, 1)
            nc.gpsimd.memset(minus_half[:], -0.5).then_inc(const_step, 1)
            nc.gpsimd.memset(before[:], 1.0).then_inc(const_step, 1)
            nc.gpsimd.iota(iota_f[:], pattern=[[1, P]], base=0, channel_multiplier=0,
                           allow_small_or_imprecise_dtypes=True).then_inc(const_step, 1)
            nc.gpsimd.iota(eidx[:], pattern=[[0, NT], [1, E]], base=0, channel_multiplier=0,
                           allow_small_or_imprecise_dtypes=True).then_inc(const_step, 1)
            pl.wait_ge(const_step, 10)
            nc.gpsimd.affine_select(out=ident[:], in_=ident[:], compare_op=ALU.not_equal, fill=1.0, base=0,
                                    pattern=[[-1, P]], channel_multiplier=1).then_inc(const_ready, 1)
            nc.gpsimd.affine_select(out=causal[:, P:], in_=causal[:, P:], compare_op=ALU.is_ge, fill=NEG, base=0,
                                    pattern=[[-1, P]], channel_multiplier=1).then_inc(const_ready, 1)
            for m, fill in ((cmask, 0.0), (cneg, NEG)):
                nc.gpsimd.affine_select(out=m[:], in_=m[:], compare_op=ALU.is_ge, fill=fill,
                                        base=-(CMP_BLOCK - 1), pattern=[[P, NT], [-CMP_STRIDE, NCMP]],
                                        channel_multiplier=1).then_inc(const_ready, 1)
            nc.gpsimd.affine_select(out=before[:], in_=before[:], compare_op=ALU.is_ge, fill=0.0, base=-1,
                                    pattern=[[1, P]], channel_multiplier=-1).then_inc(const_ready, 1)
            for n, p0 in enumerate((0, HD)):
                pl.wait_ge(const_ready, 5 + n)
                blk = group_mean[p0:p0 + HD, HD - p0:2 * HD - p0]
                nc.gpsimd.memset(blk, 0.0).then_inc(const_ready, 1)
            pl.wait_ge(const_ready, 7)
            nc.gpsimd.memset(u[:, :, 0:PAD], 0.0).then_inc(pads_ready, 1)
            nc.gpsimd.memset(cp[:], 0.0).then_inc(pads_ready, 1)

            for l in range(L):
                for m in (2 * l, 2 * l + 1):
                    if m % 2 == 0:
                        for i in range(NT):
                            pl.wait_ge(ms_ready, NT * m + i + 1)
                            nc.gpsimd.tensor_tensor(rms[:, i:i + 1], ss[:, i:i + 1], minus_half[:, 0:1],
                                                    ALU.pow).then_inc(rms_ready, 1)
                        pl.wait_ge(stat_ready, l + 1)
                        nc.gpsimd.tensor_tensor(rstat[:], stat[:], minus_half[:], ALU.pow).then_inc(rstat_ready, 1)
                        pl.wait_ge(rstat_ready, l + 1)
                        pl.wait_ge(cstat_ready, l + 1)
                        nc.gpsimd.tensor_tensor(cstat[0:MC, 1:2], cstat[0:MC, 0:1], minus_half[0:MC, 0:1],
                                                ALU.pow).then_inc(rcstat_ready, 1)
                    else:
                        pl.wait_ge(rcstat_ready, l + 1)
                        pl.wait_ge(centred_ready, 2 * (l + 1))
                        nc.gpsimd.tensor_tensor(u[:, :, PAD:], y[:], y[:], ALU.mult).then_inc(squares_ready, 1)
                        pl.wait_ge(squares_ready, l + 1)
                        for i in range(NT):
                            pl.wait_ge(ms_ready, NT * m + i + 1)
                            nc.gpsimd.tensor_tensor(rms[:, i:i + 1], ss[:, i:i + 1], minus_half[:, 0:1],
                                                    ALU.pow).then_inc(rms_ready, 1)

        @block.scalar
        def _(sc):
            sc.dma_start(par[:], small.rearrange("l p n -> p l n")).then_inc(par_loaded, 16)
            sc.dma_start(rows_sb[0:33:32, :], rows[:, :]).then_inc(par_loaded, 16)
            sc.dma_start(router_sb[:], router.rearrange("(k p) e -> p k e", p=P)).then_inc(par_loaded, 16)

            def p_(l, name, i=0, n=1):
                return par[:, l, col[name] + i:col[name] + i + n]

            def square_sums(m):
                if m == 0:
                    sc.wait_ge(x_loaded, 16 * NT)
                for i in range(NT):
                    if m > 0:
                        sc.wait_ge(x_ready, 4 * (m - 1) + NH * (i + 1))
                    nc.scalar.activation(hn[:, i, :], x_sb[:, i, :], ACT.Square,
                                         accum_out=ss[:, i:i + 1]).then_inc(ss_ready, 1)

            def high_part(t, j=0):
                wait_raw(sc, t, j)
                if t >= SPLIT:
                    sc.wait_ge(w_used, j * XS + (t - SPLIT + 1))
                nc.scalar.copy(w_hi[t % SPLIT][:], raw(t)).then_inc(w_hi_ready, 1)

            for l in range(L):
                square_sums(2 * l)
                if l == 0:
                    sc.wait_ge(par_loaded, 48)
                for c in range(CC):
                    sc.wait_ge(glu_psum, CC * l + c + 1)
                    if c >= 2:
                        sc.wait_ge(u_ready, CC * l + c - 1)
                    nc.scalar.activation(sig[:, c % 2, :], bank[c % 2][:, S:2 * S], ACT.Sigmoid).then_inc(sig_ready, 1)
                for n in range(6):
                    c, i = divmod(n, NT)
                    w = min(BANK, ZA - c * BANK)
                    sc.wait_ge(z_psum, 6 * l + n + 1)
                    nc.scalar.copy(z[:, i, c * BANK:c * BANK + w], bank[2 + n][:, 0:w]).then_inc(z_ready, 1)
                sc.wait_ge(z_ready, 6 * l + 6)
                for i in range(NT):
                    nc.scalar.activation(gates[:, i, :], z[:, i, GL0:GL0 + 3 * H], ACT.Sigmoid).then_inc(gates_ready, 1)
                for a in range(2):
                    sc.wait_ge(hid_psum, 2 * l + a + 1)
                    nc.scalar.activation(hid[0:MC, a, :], bank[5 + a][0:MC, 0:HID], ACT.Silu).then_inc(hid_ready, 1)
                sc.wait_ge(hidT_psum, l + 1)
                nc.scalar.copy(hidT[:, :, 0:MC],
                               bank[7][:, 0:4 * 2 * CPAD].rearrange("p (a n) -> p a n", a=4)[:, :, 0:MC]) \
                    .then_inc(hidT_ready, 1)
                sc.wait_ge(cmp_psum, 2 * l + 2)
                nc.scalar.copy(vc[0:MC, :], bank[6][0:MC, 0:HD]).then_inc(vc_ready, 1)

                def exponentials(n):
                    gi, kv, i, b, h0, nh = units[n]
                    keys = (i + 1) * P
                    sc.wait_ge(s_ready, NU * l + n + 1)
                    if n >= 2:
                        sc.wait_ge(pT_psum, NU * l + n - 1)
                    for h in range(nh):
                        nc.scalar.activation(probs[:, n % 2, h * keys:(h + 1) * keys],
                                             scores[:, n % 2, h * keys:(h + 1) * keys], ACT.Exp,
                                             bias=negmax[:, n % 2, h:h + 1],
                                             accum_out=psumr[:, n % 2, h:h + 1]).then_inc(exp_ready, 1)

                exponentials(0)
                exponentials(1)
                sc.wait_ge(cs_ready, l + 1)
                for i in range(NT):
                    nc.scalar.activation(cp[:, i, :, :, 0:NCMP], cp[:, i, :, :, 0:NCMP], ACT.Exp).then_inc(cexp_ready, 1)

                def evacuate_cpT():
                    sc.wait_ge(cpT_psum, l + 1)
                    for i in range(NT):
                        nc.scalar.copy(cpT[0:2 * CPAD, i, :], bank[6 + i][0:2 * CPAD, :]).then_inc(cpT_ready, 1)

                def evacuate_pT(n):
                    gi, kv, i, b, h0, nh = units[n]
                    sc.wait_ge(pT_psum, NU * l + n + 1)
                    if gi >= 2:
                        sc.wait_ge(o_psum, 4 * l + gi - 1)
                    dst = probsT[:, gi % 2, b, 0:i + 1, h0 * P:(h0 + nh) * P]
                    src = bank[2 + n % 2][:].rearrange("p (k n) -> p k n", k=i + 1)
                    nc.scalar.copy(dst, src).then_inc(pT_ready, 1)

                def evacuate_o(gi):
                    kv, i = groups[gi]
                    sc.wait_ge(o_psum, 4 * l + gi + 1)
                    r = slice(kv * HD, (kv + 1) * HD)
                    nc.scalar.copy(mixT[r, CC:CC + G, i * P:(i + 1) * P],
                                   bank[4 + i][r, :].rearrange("p (g t) -> p g t", g=G)).then_inc(mix_ready, 1)

                for n in range(NU + 1):
                    if n < NU:
                        if n >= 2:
                            exponentials(n)
                    else:
                        sc.wait_ge(rvar_ready, CC * (l + 1))
                        nc.scalar.activation(u[:, :, PAD:], u[:, :, PAD:], ACT.Sqrt).then_inc(std_ready, 1)
                    if n == 0:
                        evacuate_cpT()
                    if n >= 1:
                        evacuate_pT(n - 1)
                        for gi in range(len(groups)):
                            if n - 1 == group_last[gi] + 1:
                                evacuate_o(gi)
                sc.wait_ge(yn_ready, l + 1)
                for c in range(CC):
                    nc.scalar.activation(mixT[:, c, :], y[:, c, :], ACT.Silu, scale=p_(l, "ln_g", c),
                                         bias=p_(l, "ln_b", c)).then_inc(conv_mix, 1)
                evacuate_o(len(groups) - 1)
                square_sums(2 * l + 1)
                if l == 0:
                    for q in range(4):
                        i, h = divmod(q, 2)
                        sc.wait_ge(hT_ready, 4 * (2 * l + 1) + q + 1)
                        nc.scalar.copy(hT_hi[:, 4 * h:4 * h + 4, i * P:(i + 1) * P],
                                       hT[:, 4 * h:4 * h + 4, i * P:(i + 1) * P]).then_inc(hTs_hi, 1)
                    high_part(piece_of["d1", 0, 0])
                    high_part(piece_of["d3", 0, 0])
                    for g in range(NDG + 1):
                        if g >= 1:
                            sc.wait_ge(dact_ready, g)
                            if g >= 2:
                                sc.wait_ge(w_used, piece_of["d2", 0, g - 2] + 1)
                            nc.scalar.copy(dact_hi[:].rearrange("p a t -> p (a t)"),
                                           dact[:, (g - 1) % 2, :]).then_inc(dact_hi_ready, 1)
                            high_part(piece_of["d2", 0, g - 1])
                        if g < NDG:
                            sc.wait_ge(w_used, piece_of["d1", 0, g] + 1)
                            if g >= 2:
                                sc.wait_ge(dact_ready, g - 1)
                            nc.scalar.activation(dsg[:, g % 2, :], bank[4 + g % 2][:], ACT.Silu).then_inc(dsg_ready, 1)
                        if g + 1 < NDG:
                            high_part(piece_of["d1", 0, g + 1])
                            high_part(piece_of["d3", 0, g + 1])

            sc.wait_ge(lse_ready, 1)
            nc.scalar.activation(rv[:, 3, :], rv[:, 2, :], ACT.Exp).then_inc(lexp_ready, 1)
            for q in range(4):
                i, h = divmod(q, 2)
                sc.wait_ge(hback_psum, q + 1)
                nc.scalar.copy(h_hi[:, i, h * BANK:(h + 1) * BANK], bank[4 + q][:]).then_inc(h_hi_ready, 1)

            def gathered_high(count):
                for h in range(2):
                    sc.wait_ge(xe_psum, count + h + 1)
                    nc.scalar.copy(xe_hi[:, 4 * h:4 * h + 4, :], bank[1 + 2 * h][:].rearrange("p (k s) -> p k s", k=4)) \
                        .then_inc(xe_hi_ready, 1)

            gathered_high(0)
            sc.wait_ge(trips_ready, 1)
            trips = sc.value_load(trips_i[0:1, 0:1], min_val=E, max_val=PASSES * E)
            with sc.Fori(0, trips) as j:
                def used(kind, c, half=1):
                    sc.wait_ge(w_used, j * XS + (BASE + xplace[kind, c, half] + 1))

                def actT_high(c):
                    sc.wait_ge(actT_psum, j * FCH + c + 1)
                    nc.scalar.copy(actT_hi[:], bank[4][:]).then_inc(actT_hi_ready, 1)

                done = 0
                for c in range(FCH):
                    e1_end = xplace["e1", c, 1]
                    while done <= min(e1_end + SPLIT, XS - 1):
                        high_part(BASE + done, j)
                        done += 1
                    if c >= 1:
                        actT_high(c - 1)
                    used("e1", c)
                    if c >= 2:
                        sc.wait_ge(act_ready, j * FCH + c - 1)
                    nc.scalar.activation(sg[:, c % 2, :], bank[c % 2][:], ACT.Silu).then_inc(sg_ready, 1)
                    if c == 3:
                        sc.wait_ge(selT_psum, j + 1)
                        nc.scalar.copy(selT[:], bank[7][:, 0:S]).then_inc(selT_ready, 1)
                        nc.scalar.copy(slot_weight[:], bank[7][:, S:S + 1]).then_inc(selT_ready, 1)
                while done < XS:
                    high_part(BASE + done, j)
                    done += 1
                gathered_high(j * 4 + 4)
                actT_high(FCH - 1)
                used("e2", FCH - 1)
                sc.wait_ge(selT_ready, (j + 1) * 2)
                for n in range(NH):
                    nc.scalar.activation(ye_hi[:, n * BANK:(n + 1) * BANK], bank[5 + n][:], ACT.Copy,
                                         scale=slot_weight[:, 0:1]).then_inc(ye_hi_ready, 1)

        @block.vector
        def _(dv):
            steps = [0]

            def link(ins):
                steps[0] += 1
                ins.then_inc(dve_step, 1)
                dv.wait_ge(dve_step, steps[0])

            V = nc.vector

            def p_(l, name, i=0, n=1):
                return par[:, l, col[name] + i:col[name] + i + n]

            dv.wait_ge(const_ready, 7)
            dv.wait_ge(pads_ready, 2)

            def normalise(m, products=None):
                l, ffn = divmod(m, 2)
                for i in range(NT):
                    for n in range(NH if m > 0 else 0):
                        if products is not None:
                            dv.wait_ge(products, 4 * l + NH * i + n + 1)
                        add_to_x(2 * n + i, i, n).then_inc(x_ready, 1)
                    dv.wait_ge(ss_ready, NT * m + i + 1)
                    V.tensor_scalar(ss[:, i:i + 1], ss[:, i:i + 1], 1.0 / D, EPS, ALU.mult, ALU.add).then_inc(ms_ready, 1)
                    dv.wait_ge(rms_ready, NT * m + i + 1)
                    V.tensor_scalar(hn[:, i, :], x_sb[:, i, :], rms[:, i:i + 1], None, ALU.mult).then_inc(hn_ready, 1)
                if m == 0:
                    dv.wait_ge(par_loaded, 48)
                gain = p_(l, "ffn_g" if ffn else "attn_g", 0, KD)
                for q in range(4):
                    i, h = divmod(q, 2)
                    dv.wait_ge(hT_psum, 4 * m + q + 1)
                    V.tensor_tensor(hT[:, 4 * h:4 * h + 4, i * P:(i + 1) * P],
                                    bank[4 + q][:].rearrange("p (k t) -> p k t", k=4),
                                    gain[:, 4 * h:4 * h + 4].unsqueeze(2).to_broadcast([P, 4, P]),
                                    ALU.mult).then_inc(hT_ready, 1)

            def add_to_x(b, i, n):
                part = x_sb[:, i, n * BANK:(n + 1) * BANK]
                return V.tensor_tensor(part, part, bank[b][:], ALU.add)

            def low_part(t, j=0):
                dv.wait_ge(w_hi_ready, j * XS + (t + 1))
                V.tensor_tensor(w_lo[t % SPLIT][:], raw(t), w_hi[t % SPLIT][:].bitcast(F32),
                                ALU.subtract).then_inc(w_lo_ready, 1)

            conv_n = [0]
            TAP_A, TAP_B = 20, 26

            for l in range(L):
                if l == 0:
                    normalise(0)

                def glu(c):
                    dv.wait_ge(sig_ready, CC * l + c + 1)
                    V.tensor_tensor(u[:, c, PAD:], bank[c % 2][:, 0:S], sig[:, c % 2, :], ALU.mult).then_inc(u_ready, 1)

                def conv_taps(c0, taps):
                    for tap in taps:
                        for c in (c0, c0 + 1):
                            w = p_(l, "conv_w", c * TAPS + tap)
                            if tap == 0:
                                V.tensor_scalar(y[:, c, :], u[:, c, 0:S], w, p_(l, "conv_b", c), ALU.mult,
                                                ALU.add).then_inc(conv_step, 1)
                            else:
                                dv.wait_ge(conv_step, conv_n[0] - 1)
                                V.scalar_tensor_tensor(out=y[:, c, :], in0=u[:, c, tap:tap + S], scalar=w,
                                                       in1=y[:, c, :], op0=ALU.mult,
                                                       op1=ALU.add).then_inc(conv_step, 1)
                            conv_n[0] += 1

                glu(0)
                glu(1)
                dv.wait_ge(u_ready, CC * l + 2)
                conv_taps(0, range(9))
                glu(2)
                conv_taps(0, range(9, 17))
                glu(3)
                conv_taps(0, range(17, TAPS))
                dv.wait_ge(u_ready, CC * l + 4)
                conv_taps(2, range(TAP_A))
                dv.wait_ge(z_ready, 6 * (l + 1))
                for i in range(NT):
                    src = z[:, i, KC0:KC0 + 4 * HD].rearrange("p (a d) -> p a d", a=4)
                    V.tensor_copy(zdup[:, i], src.unsqueeze(2).to_broadcast([P, 4, 2, HD])).then_inc(zdup_ready, 1)
                link(V.memset(blkT[:], 0.0))
                for a in range(2):
                    dv.wait_ge(zdup_psum, 2 * l + a + 1)
                    for kv in range(KV):
                        for q in range(2):
                            r = slice(q * HD, (q + 1) * HD)
                            src = bank[3 + a][r, kv * S:(kv + 1) * S].rearrange("p (c o e) -> p c o e", e=2, o=8)
                            for half in range(2):
                                dst = blkT[r, a, 8 * half:8 * half + 8, kv * CPAD:kv * CPAD + NCMP]
                                V.tensor_tensor(dst, src[:, half:half + NCMP, :, q].rearrange("p c o -> p o c"),
                                                par[r, l, col["pos"] + a * LP + 8 * half:
                                                    col["pos"] + a * LP + 8 * half + 8].unsqueeze(2)
                                                .to_broadcast([HD, 8, NCMP]), ALU.add).then_inc(blk_ready, 1)
                for i in range(NT):
                    zq = z[:, i, 0:AW]
                    link(V.tensor_tensor(sq[:, 0:AW], zq, zq, ALU.mult))
                    zk = z[:, i, KS0:KS0 + 4 * P].rearrange("p (b c) -> p b c", b=2)[:, :, 0:P]
                    link(V.tensor_tensor(sq[:, AW:AW + 2 * P].rearrange("p (b c) -> p b c", b=2), zk, zk, ALU.mult))
                    link(V.tensor_reduce(stat[:, i * 12:(i + 1) * 12],
                                         sq[:, 0:AW + 2 * P].rearrange("p (h d) -> p h d", d=HD), AX_X, ALU.add))
                V.tensor_scalar(stat[:], stat[:], 1.0 / HD, EPS, ALU.mult, ALU.add).then_inc(stat_ready, 1)
                conv_taps(2, range(TAP_A, TAP_B))
                dv.wait_ge(rstat_ready, l + 1)
                for i in range(NT):
                    rs = rstat[:, i * 12:i * 12 + 8].rearrange("p (k g) -> p k g", k=KV)
                    for kv in range(KV):
                        V.tensor_tensor(qn[:, i, :, kv, :],
                                        z[:, i, kv * G * HD:(kv + 1) * G * HD].rearrange("p (g d) -> p g d", g=G),
                                        rs[:, kv, :].unsqueeze(2).to_broadcast([P, G, HD]),
                                        ALU.mult).then_inc(qkn_ready, 1)
                    for b in range(2):
                        k0 = KS0 + b * 2 * P
                        V.tensor_tensor(kn[:, i, b], z[:, i, k0:k0 + P].rearrange("p (k d) -> p k d", k=KV),
                                        rstat[:, i * 12 + 8 + 2 * b:i * 12 + 10 + 2 * b].unsqueeze(2)
                                        .to_broadcast([P, KV, HD]), ALU.mult).then_inc(qkn_ready, 1)
                for i in range(NT):
                    dv.wait_ge(qkT_psum, 3 * l + i + 1)
                    V.tensor_scalar(qT[:, :, i * P:(i + 1) * P], bank[i][:].rearrange("p (g t) -> p g t", g=G),
                                    p_(l, "q_g"), HD ** -0.5, ALU.mult, ALU.mult).then_inc(qkT_ready, 1)
                dv.wait_ge(qkT_psum, 3 * l + 3)
                for b in range(2):
                    V.tensor_scalar(kT[:, b, :], bank[2][:, b * S:(b + 1) * S], p_(l, "k_g", 1 + b), None,
                                    ALU.mult).then_inc(qkT_ready, 1)

                def masked_scores(n):
                    gi, kv, i, b, h0, nh = units[n]
                    keys = (i + 1) * P
                    dv.wait_ge(s_psum, NU * l + n + 1)
                    if n >= 2:
                        dv.wait_ge(exp_ready, exp_count(l, n - 2))
                    s3 = scores[:, n % 2, :].rearrange("p (h k) -> p h k", h=nh)
                    link(V.tensor_tensor(s3, bank[n % 2][:].rearrange("p (h k) -> p h k", h=nh),
                                         causal[:, 2 * P - keys:].unsqueeze(1).to_broadcast([P, nh, keys]), ALU.add))
                    V.tensor_reduce(negmax[:, n % 2, 0:nh], s3, AX_X, ALU.max, negate=True).then_inc(s_ready, 1)

                conv_taps(2, range(TAP_B, TAPS))
                masked_scores(0)
                masked_scores(1)
                dv.wait_ge(cmp_psum, 2 * l + 1)
                link(V.tensor_copy(kcn[0:MC, 0, :], bank[5][0:MC, 0:HD]))
                link(V.tensor_tensor(kcn[0:MC, 1, :], kcn[0:MC, 0, :], kcn[0:MC, 0, :], ALU.mult))
                link(V.tensor_reduce(cstat[0:MC, 0:1], kcn[0:MC, 1, :], AX_X, ALU.add))
                V.tensor_scalar(cstat[0:MC, 0:1], cstat[0:MC, 0:1], 1.0 / HD, EPS, ALU.mult, ALU.add) \
                    .then_inc(cstat_ready, 1)
                dv.wait_ge(rcstat_ready, l + 1)
                link(V.tensor_scalar(kcn[0:MC, 0, :], kcn[0:MC, 0, :], cstat[0:MC, 1:2], None, ALU.mult))
                V.tensor_copy(kcn[0:MC, 1, :], kcn[0:MC, 0, :]).then_inc(kcn_ready, 1)
                dv.wait_ge(kcT_psum, l + 1)
                V.tensor_scalar(kcT[:], bank[7][:, 0:MC], p_(l, "k_g", 0), None, ALU.mult).then_inc(kcT_ready, 1)
                dv.wait_ge(cs_psum, KV * (l + 1))
                cpv = cp[:].rearrange("p i g k c -> p i (g k) c")[:, :, :, 0:NCMP]
                cflat = cp[:].rearrange("p i g k c -> p (i g k) c")[:, :, 0:NCMP]
                for kv in range(KV):
                    cps = bank[6 + kv][:, 0:NT * G * CPAD].rearrange("p (i g c) -> p i g c", i=NT, g=G)
                    for i in range(NT):
                        link(V.tensor_tensor(cp[:, i, :, kv, 0:NCMP], cps[:, i, :, 0:NCMP],
                                             cneg[:, i, :].unsqueeze(1).to_broadcast([P, G, NCMP]), ALU.add))
                link(V.tensor_reduce(cmx[:], cflat, AX_X, ALU.max))
                V.tensor_tensor(cflat, cflat, cmx[:].unsqueeze(2).to_broadcast([P, NT * H, NCMP]),
                                ALU.subtract).then_inc(cs_ready, 1)
                dv.wait_ge(cexp_ready, NT * (l + 1))
                for i in range(NT):
                    link(V.tensor_tensor(cpv[:, i], cpv[:, i], cmask[:, i, :].unsqueeze(1).to_broadcast([P, H, NCMP]),
                                         ALU.mult))
                link(V.tensor_reduce(csum[:], cflat, AX_X, ALU.add))
                link(V.tensor_scalar(csum[:], csum[:], 1e-30, None, ALU.max))
                link(V.reciprocal(csum[:], csum[:]))
                dv.wait_ge(gates_ready, NT * (l + 1))
                for i in range(NT):
                    gv = gates[:, i, :].rearrange("p (k g b) -> p g k b", k=KV, g=G)[:, :, :, 0]
                    link(V.tensor_tensor(crs[:, i * H:(i + 1) * H].rearrange("p (g k) -> p g k", g=G),
                                         csum[:, i * H:(i + 1) * H].rearrange("p (g k) -> p g k", g=G), gv, ALU.mult))
                V.tensor_tensor(cflat, cflat, crs[:].unsqueeze(2).to_broadcast([P, NT * H, NCMP]),
                                ALU.mult).then_inc(cp_ready, 1)
                for n in range(NU):
                    if 1 < n + 1 < NU:
                        masked_scores(n + 1)
                    gi, kv, i, b, h0, nh = units[n]
                    keys = (i + 1) * P
                    dv.wait_ge(exp_ready, exp_count(l, n))
                    link(V.reciprocal(pscale[:, n % 2, 0:nh], psumr[:, n % 2, 0:nh]))
                    gv = gates[:, i, :].rearrange("p (h b) -> p h b", b=3)[:, kv * G + h0:kv * G + h0 + nh, 1 + b]
                    link(V.tensor_tensor(pscale[:, n % 2, 0:nh], pscale[:, n % 2, 0:nh], gv, ALU.mult))
                    p3 = probs[:, n % 2, :].rearrange("p (h k) -> p h k", h=nh)
                    V.tensor_tensor(p3, p3, pscale[:, n % 2, 0:nh].unsqueeze(2).to_broadcast([P, nh, keys]),
                                    ALU.mult).then_inc(p_ready, 1)
                    if n == 2:
                        for h in range(2):
                            dv.wait_ge(mean_psum, 2 * l + h + 1)
                            part = y[:, 2 * h:2 * h + 2, :]
                            V.tensor_tensor(part, part, bank[6 + h][:].rearrange("p (c t) -> p c t", c=2),
                                            ALU.subtract).then_inc(centred_ready, 1)
                    if n == 6:
                        dv.wait_ge(var_psum, 2 * l + 2)
                        for h in range(2):
                            link(V.tensor_scalar(u[:, 2 * h:2 * h + 2, PAD:],
                                                 bank[6 + h][:].rearrange("p (c t) -> p c t", c=2),
                                                 EPS, None, ALU.add))
                    if 7 <= n < 7 + CC:
                        V.reciprocal(u[:, n - 7, PAD:], u[:, n - 7, PAD:]).then_inc(rvar_ready, 1)
                dv.wait_ge(std_ready, l + 1)
                V.tensor_tensor(y[:], y[:], u[:, :, PAD:], ALU.mult).then_inc(yn_ready, 1)
                normalise(2 * l + 1, wo_psum)
                if l == 0:
                    for q in range(4):
                        i, h = divmod(q, 2)
                        part = (slice(None), slice(4 * h, 4 * h + 4), slice(i * P, (i + 1) * P))
                        dv.wait_ge(hTs_hi, q + 1)
                        V.tensor_tensor(hT_lo[part], hT[part], hT_hi[part].bitcast(F32), ALU.subtract) \
                            .then_inc(hTs_ready, 1)
                    low_part(piece_of["d1", 0, 0])
                    low_part(piece_of["d3", 0, 0])
                    for g in range(NDG + 1):
                        if g >= 1:
                            dv.wait_ge(dact_hi_ready, g)
                            V.tensor_tensor(dact_lo[:].rearrange("p a t -> p (a t)"), dact[:, (g - 1) % 2, :],
                                            dact_hi[:].rearrange("p a t -> p (a t)").bitcast(F32), ALU.subtract) \
                                .then_inc(dact_lo_ready, 1)
                            low_part(piece_of["d2", 0, g - 1])
                        if g + 1 < NDG:
                            low_part(piece_of["d1", 0, g + 1])
                        if g < NDG:
                            dv.wait_ge(dsg_ready, g + 1)
                            dv.wait_ge(w_used, piece_of["d3", 0, g] + 1)
                            V.tensor_tensor(dact[:, g % 2, :], dsg[:, g % 2, :], bank[6 + g % 2][:],
                                            ALU.mult).then_inc(dact_ready, 1)
                        if g + 1 < NDG:
                            low_part(piece_of["d3", 0, g + 1])
                    dv.wait_ge(w_used, BASE)
                    normalise(2 * l + 2)

            def r_(a):
                return rt[:, a]

            def bc(v):
                return v.unsqueeze(2).to_broadcast([P, NT, E])

            dv.wait_ge(logit_psum, 1)
            link(V.tensor_copy(r_(0), bank[0][:, 0:NT * E].rearrange("p (i e) -> p i e", i=NT)))

            def first_max(logit, top, onehot, tmp, idx):
                link(V.tensor_reduce(top, r_(logit), AX_X, ALU.max))
                link(V.tensor_tensor(r_(tmp), r_(logit), bc(top), ALU.is_equal))
                link(V.scalar_tensor_tensor(out=r_(tmp), in0=r_(tmp), scalar=-float(E), in1=eidx[:],
                                            op0=ALU.mult, op1=ALU.add))
                link(V.tensor_reduce(idx, r_(tmp), AX_X, ALU.min))
                link(V.tensor_scalar(idx, idx, float(E), None, ALU.add))
                link(V.tensor_tensor(r_(onehot), eidx[:], bc(idx), ALU.is_equal))

            first_max(0, rv[:, 0, :], 1, 2, rv[:, 4, :])
            link(V.scalar_tensor_tensor(out=r_(3), in0=r_(1), scalar=-3e38, in1=r_(0), op0=ALU.mult, op1=ALU.add))
            first_max(3, rv[:, 1, :], 4, 2, rv[:, 5, :])
            V.tensor_tensor(rv[:, 2, :], rv[:, 1, :], rv[:, 0, :], ALU.subtract).then_inc(lse_ready, 1)
            V.tensor_tensor(r_(5), r_(1), r_(4), ALU.add).then_inc(chosen_ready, 1)
            dv.wait_ge(lexp_ready, 1)
            link(V.tensor_scalar(rv[:, 6, :], rv[:, 3, :], 1.0, None, ALU.add))
            link(V.reciprocal(rv[:, 6, :], rv[:, 6, :]))
            link(V.tensor_tensor(rv[:, 7, :], rv[:, 6, :], rv[:, 3, :], ALU.mult))
            link(V.tensor_tensor(r_(6), r_(1), bc(rv[:, 6, :]), ALU.mult))
            link(V.tensor_tensor(r_(7), r_(4), bc(rv[:, 7, :]), ALU.mult))
            for q in range(PASSES):
                link(V.tensor_tensor(wgt_tab[:, :, q * E:(q + 1) * E], r_(6), r_(7), ALU.add))
            dv.wait_ge(pos_psum, 1)
            link(V.tensor_scalar(r_(8), r_(5), float(4 * S), -float(4 * S), ALU.mult, ALU.add))
            link(V.tensor_tensor(pos_tab[:, :, 0:E], r_(8), bank[1][:, 0:NT * E].rearrange("p (i e) -> p i e", i=NT),
                                 ALU.add))
            for q in range(1, PASSES):
                link(V.tensor_scalar(pos_tab[:, :, q * E:(q + 1) * E], pos_tab[:, :, 0:E], -float(q * CAP), None,
                                     ALU.add))
            link(V.memset(pos_tab[:, :, PASSES * E:], -1.0))
            link(V.tensor_reduce(mcount[:, 0:1], bank[1][:, NT * E:NT * E + E], AX_X, ALU.max))
            link(V.tensor_scalar(mcount[:, 0:1], mcount[:, 0:1], float(CAP), float(E), ALU.is_gt, ALU.mult))
            link(V.tensor_scalar(mcount[:, 0:1], mcount[:, 0:1], float(E), None, ALU.add))
            V.tensor_copy(trips_i[:], mcount[:, 0:1]).then_inc(trips_ready, 1)
            dv.wait_ge(trips_ready, 1)

            def select(j):
                for i in range(NT):
                    where = pos_tab[:, i, bass.ds(j, 1)]
                    V.tensor_scalar(sel[:, i, :], iota_f[:], where, None, ALU.is_equal).then_inc(sel_ready, 1)
                    V.tensor_scalar(sel_f[:, i, :], iota_f[:], where, None, ALU.is_equal).then_inc(self_ready, 1)

            def gathered_low(count):
                for h in range(2):
                    dv.wait_ge(xe_psum, count + 3 + h)
                    V.tensor_copy(xe_lo[:, 4 * h:4 * h + 4, :],
                                  bank[7 - 6 * h][:].rearrange("p (k s) -> p k s", k=4)).then_inc(xe_lo_ready, 1)

            select(0)
            for q in range(4):
                i, h = divmod(q, 2)
                dv.wait_ge(h_hi_ready, q + 1)
                V.tensor_tensor(h_lo[:, i, h * BANK:(h + 1) * BANK], bank[4 + q][:],
                                h_hi[:, i, h * BANK:(h + 1) * BANK].bitcast(F32), ALU.subtract).then_inc(h_split, 1)
            V.memset(mcount[:, 0:1], 0.0).then_inc(added, 1)
            gathered_low(0)
            trips = dv.value_load(trips_i[0:1, 0:1], min_val=E, max_val=PASSES * E)
            with dv.Fori(0, trips) as j:
                def used(kind, c, half=1):
                    dv.wait_ge(w_used, j * XS + (BASE + xplace[kind, c, half] + 1))

                def actT_low(c):
                    dv.wait_ge(actT_hi_ready, j * FCH + c + 1)
                    V.tensor_tensor(actT_lo[:], bank[4][:], actT_hi[:].bitcast(F32), ALU.subtract) \
                        .then_inc(actT_ready, 1)

                done = 0
                for c in range(FCH):
                    e1_end = xplace["e1", c, 1]
                    while done <= min(e1_end + SPLIT, XS - 1):
                        low_part(BASE + done, j)
                        done += 1
                    if c >= 1:
                        actT_low(c - 1)
                    if done < XS:
                        low_part(BASE + done, j)
                        done += 1
                    dv.wait_ge(sg_ready, j * FCH + c + 1)
                    used("e3", c)
                    V.tensor_tensor(act[:, c % 2, :], sg[:, c % 2, :], bank[2 + c % 2][:],
                                    ALU.mult).then_inc(act_ready, 1)
                    if c == 3:
                        dv.wait_ge(selT_psum, j + 1)
                        select(j + 1)
                while done < XS:
                    low_part(BASE + done, j)
                    done += 1
                actT_low(FCH - 1)
                gathered_low(j * 4 + 4)
                dv.wait_ge(selT_ready, (j + 1) * 2)
                for n in range(NH):
                    dv.wait_ge(ye_hi_ready, j * NH + n + 1)
                    V.scalar_tensor_tensor(out=ye_lo[:, n * BANK:(n + 1) * BANK], in0=bank[5 + n][:],
                                           scalar=slot_weight[:, 0:1],
                                           in1=ye_hi[:, n * BANK:(n + 1) * BANK].bitcast(F32),
                                           op0=ALU.mult, op1=ALU.subtract).then_inc(ye_lo_ready, 1)
                for q, b in enumerate(BACK):
                    i, n = divmod(q, 2)
                    dv.wait_ge(back_psum, j * 4 + q + 1)
                    add_to_x(b, i, n).then_inc(added, 1)
            dv.wait_ge(added, trips * 4 + 1)
            V.memset(cmx[:], 0.0).then_inc(trips_done, 1)

        @block.tensor
        def _(pe):
            T = nc.tensor
            pe.wait_ge(const_ready, 7)

            def transpose_rows(m):
                for i in range(NT):
                    pe.wait_ge(hn_ready, NT * m + i + 1)
                    for h in range(2):
                        for k in range(4):
                            last = T.transpose(bank[4 + 2 * i + h][:, k * P:(k + 1) * P],
                                               hn[:, i, (4 * h + k) * P:(4 * h + k + 1) * P], ident[:])
                        last.then_inc(hT_psum, 1)
                pe.wait_ge(hT_ready, 4 * (m + 1))

            def product(dst, lhs, rhs, chunks):
                for n, k in enumerate(chunks):
                    last = T.matmul(dst, lhs(k), rhs(k), start=(n == 0), stop=(n == len(chunks) - 1))
                return last

            for l in range(L):
                transpose_rows(2 * l)
                wait_slot(pe, "win", l, 0)
                wait_slot(pe, "win", l, 1)
                for c in range(CC):
                    if c >= 2:
                        pe.wait_ge(u_ready, CC * l + c - 1)
                    for half in range(2):
                        w = view("win", l, half)
                        last = product(bank[c % 2][:, half * S:(half + 1) * S],
                                       lambda k: w[:, k, c * P:(c + 1) * P], lambda k: hT[:, k, :], range(KD))
                    last.then_inc(glu_psum, 1)
                for n in range(6):
                    c, i = divmod(n, NT)
                    if i == 0:
                        wait_slot(pe, "win", l, 2 + c)
                    w = view("win", l, 2 + c)
                    product(bank[2 + n][:, 0:w.shape[2]], lambda k: hT[:, k, i * P:(i + 1) * P],
                            lambda k: w[:, k, :], range(KD)).then_inc(z_psum, 1)
                pe.wait_ge(zdup_ready, NT * (l + 1))
                for a in range(2):
                    for kv in range(KV):
                        for i in range(NT):
                            last = T.transpose(bank[3 + a][:, kv * S + i * P:kv * S + (i + 1) * P],
                                               zdup[:, i, 2 * a + kv].rearrange("p e d -> p (e d)"), ident[:])
                    last.then_inc(zdup_psum, 1)
                r0 = 32 * l
                pe.wait_ge(par_loaded, 48)
                for a in range(2):
                    wait_slot(pe, "cmp", l, a)
                    pe.wait_ge(blk_ready, 16 * l + 8 * (a + 1))
                    w = view("cmp", l, a)
                    for k in range(LP):
                        T.matmul(bank[5 + a][0:MC, 0:HID], blkT[:, a, k, 0:MC], w[:, k, :], start=(k == 0), stop=False)
                    T.matmul(bank[5 + a][0:MC, 0:HID], ones[r0:r0 + 1, 0:MC], rows_sb[r0:r0 + 1, a * HID:(a + 1) * HID],
                             start=False, stop=True).then_inc(hid_psum, 1)
                pe.wait_ge(qkn_ready, 8 * (l + 1))
                for i in range(NT):
                    for g in range(G):
                        last = T.transpose(bank[i][:, g * P:(g + 1) * P],
                                           qn[:, i, g].rearrange("p k d -> p (k d)"), ident[:])
                    last.then_inc(qkT_psum, 1)
                for b in range(2):
                    for i in range(NT):
                        last = T.transpose(bank[2][:, b * S + i * P:b * S + (i + 1) * P],
                                           kn[:, i, b].rearrange("p k d -> p (k d)"), ident[:])
                last.then_inc(qkT_psum, 1)
                def score(n):
                    gi, kv, i, b, h0, nh = units[n]
                    keys = (i + 1) * P
                    if n >= 2:
                        pe.wait_ge(s_ready, NU * l + n - 1)
                    r = slice(kv * HD, (kv + 1) * HD)
                    for h in range(nh):
                        last = T.matmul(bank[n % 2][:, h * keys:(h + 1) * keys], qT[r, h0 + h, i * P:(i + 1) * P],
                                        kT[r, b, 0:keys], start=True, stop=True)
                    last.then_inc(s_psum, 1)

                pe.wait_ge(hid_ready, 2 * (l + 1))
                for a in range(2):
                    for k in range(2):
                        q = 2 * a + k
                        last = T.transpose(bank[7][:, q * 2 * CPAD:q * 2 * CPAD + MC],
                                           hid[0:MC, a, k * P:(k + 1) * P], ident[0:MC, 0:MC])
                last.then_inc(hidT_psum, 1)
                pe.wait_ge(qkT_ready, 4 * (l + 1))
                score(0)
                score(1)
                pe.wait_ge(hidT_ready, l + 1)
                for a in range(2):
                    for k in range(2):
                        w2 = par[:, l, col["w2"] + (2 * a + k) * HD:col["w2"] + (2 * a + k + 1) * HD]
                        T.matmul(bank[5 + a][0:MC, 0:HD], hidT[:, 2 * a + k, 0:MC], w2, start=(k == 0), stop=False)
                    T.matmul(bank[5 + a][0:MC, 0:HD], ones[r0:r0 + 1, 0:MC],
                             rows_sb[r0:r0 + 1, 2 * HID + a * HD:2 * HID + (a + 1) * HD],
                             start=False, stop=True).then_inc(cmp_psum, 1)
                pe.wait_ge(kcn_ready, l + 1)
                T.transpose(bank[7][:, 0:MC], kcn[0:MC].rearrange("p e d -> p (e d)"),
                            ident[0:MC, 0:MC]).then_inc(kcT_psum, 1)
                pe.wait_ge(kcT_ready, l + 1)
                pe.wait_ge(vc_ready, l + 1)
                for kv in range(KV):
                    r = slice(kv * HD, (kv + 1) * HD)
                    for i in range(NT):
                        for g in range(G):
                            o = (i * G + g) * CPAD
                            last = T.matmul(bank[6 + kv][:, o:o + NCMP], qT[r, g, i * P:(i + 1) * P],
                                            kcT[r, kv * CPAD:kv * CPAD + NCMP], start=True, stop=True)
                    last.then_inc(cs_psum, 1)

                def transpose_probs(n):
                    gi, kv, i, b, h0, nh = units[n]
                    keys = (i + 1) * P
                    pe.wait_ge(p_ready, NU * l + n + 1)
                    if n >= 2:
                        pe.wait_ge(pT_ready, NU * l + n - 1)
                    for k in range(i + 1):
                        for h in range(nh):
                            last = T.transpose(bank[2 + n % 2][:, (k * nh + h) * P:(k * nh + h + 1) * P],
                                               probs[:, n % 2, h * keys + k * P:h * keys + (k + 1) * P], ident[:])
                    last.then_inc(pT_psum, 1)

                def values(gi):
                    kv, i = groups[gi]
                    r = slice(kv * HD, (kv + 1) * HD)
                    c = slice(kv * CPAD, kv * CPAD + NCMP)
                    pe.wait_ge(pT_ready, NU * l + group_last[gi] + 1)
                    dst = bank[4 + i][r, :]
                    T.matmul(dst, vc[c, :], cpT[c, i, :], start=True, stop=False)
                    for b in range(2):
                        for k in range(i + 1):
                            v0 = (VS0, VW0)[b] + kv * HD
                            last = T.matmul(dst, z[:, k, v0:v0 + HD], probsT[:, gi % 2, b, k, :],
                                            start=False, stop=(b == 1 and k == i))
                    last.then_inc(o_psum, 1)

                pe.wait_ge(cp_ready, l + 1)
                for i in range(NT):
                    for g in range(G):
                        last = T.transpose(bank[6 + i][0:2 * CPAD, g * P:(g + 1) * P],
                                           cp[:, i, g].rearrange("p k c -> p (k c)"), ident[:])
                last.then_inc(cpT_psum, 1)
                pe.wait_ge(cpT_ready, NT * (l + 1))
                for n in range(NU):
                    if n + 2 < NU:
                        score(n + 2)
                    transpose_probs(n)
                    if n == 1:
                        pe.wait_ge(conv_step, CC * TAPS * (l + 1))
                        for h in range(2):
                            T.matmul(bank[6 + h][:], group_mean[:], y[:, 2 * h:2 * h + 2, :].rearrange("p c t -> p (c t)"),
                                     start=True, stop=True).then_inc(mean_psum, 1)
                    if n == 5:
                        pe.wait_ge(squares_ready, l + 1)
                        for h in range(2):
                            T.matmul(bank[6 + h][:], group_mean[:], u[:, 2 * h:2 * h + 2, PAD:],
                                     start=True, stop=True).then_inc(var_psum, 1)
                    for gi in range(len(groups)):
                        if n == group_last[gi] + 1:
                            values(gi)
                values(len(groups) - 1)
                for i in range(NT):
                    pe.wait_ge(mix_ready, 4 * l + KV * (i + 1))
                    for n in range(NH):
                        wait_slot(pe, "wout", l, n)
                        w = view("wout", l, n)
                        for k in list(range(CC, KD)) + list(range(CC)):
                            if k == 0 and n == 0 and i == 0:
                                pe.wait_ge(conv_mix, CC * (l + 1))
                            last = T.matmul(bank[2 * n + i][:], mixT[:, k, i * P:(i + 1) * P], w[:, k, :],
                                            start=(k == CC), stop=(k == CC - 1))
                        last.then_inc(wo_psum, 1)
                transpose_rows(2 * l + 1)
                if l == 0:
                    pe.wait_ge(hTs_ready, 4)

                    def up(kind, g):
                        t = piece_of[kind, 0, g]
                        pe.wait_ge(w_lo_ready, t + 1)
                        if g >= 2:
                            pe.wait_ge(dact_ready, g - 1)
                        hi, lo = split_views(t, KD)
                        for f in range(2):
                            dst = bank[(4 if kind == "d1" else 6) + g % 2][:, f * S:(f + 1) * S]
                            c = slice(f * P, (f + 1) * P)
                            for k in range(KD):
                                T.matmul(dst, hi[:, k, c], hT_hi[:, k, :], start=(k == 0), stop=False)
                                T.matmul(dst, hi[:, k, c], hT_lo[:, k, :], start=False, stop=False)
                                last = T.matmul(dst, lo[:, k, c], hT_hi[:, k, :], start=False, stop=(k == KD - 1))
                        last.then_inc(w_used, 1)

                    def down(g):
                        t = piece_of["d2", 0, g]
                        pe.wait_ge(w_lo_ready, t + 1)
                        pe.wait_ge(dact_lo_ready, g + 1)
                        hi, lo = split_views(t, 2)
                        for f in range(2):
                            first, end = g == 0 and f == 0, g == NDG - 1 and f == 1
                            for n in range(NH):
                                c = slice(n * BANK, (n + 1) * BANK)
                                for i in range(NT):
                                    dst, r = bank[2 * n + i][:], slice(i * P, (i + 1) * P)
                                    T.matmul(dst, dact_hi[:, f, r], hi[:, f, c], start=first, stop=False)
                                    T.matmul(dst, dact_hi[:, f, r], lo[:, f, c], start=False, stop=False)
                                    last = T.matmul(dst, dact_lo[:, f, r], hi[:, f, c], start=False, stop=end)
                        last.then_inc(w_used, 1)

                    for g in range(NDG):
                        up("d1", g)
                        up("d3", g)
                        if g >= 1:
                            down(g - 1)
                    down(NDG - 1)

            for i in range(NT):
                last = product(bank[0][:, i * E:(i + 1) * E], lambda k: hT[:, k, i * P:(i + 1) * P],
                               lambda k: router_sb[:, k, :], range(KD))
            last.then_inc(logit_psum, 1)
            for i in range(NT):
                for h in range(2):
                    for k in range(4):
                        last = T.transpose(bank[4 + 2 * i + h][:, k * P:(k + 1) * P],
                                           hT[:, 4 * h + k, i * P:(i + 1) * P], ident[:])
                    last.then_inc(hback_psum, 1)
            pe.wait_ge(chosen_ready, 1)
            chosen = rt[:, 5]
            T.matmul(bank[1][:, 0:E], before[:], chosen[:, 0, :], start=True, stop=True)
            T.matmul(bank[1][:, E:2 * E], ones[:], chosen[:, 0, :], start=True, stop=False)
            T.matmul(bank[1][:, E:2 * E], before[:], chosen[:, 1, :], start=False, stop=True)
            T.matmul(bank[1][:, 2 * E:3 * E], ones[:], chosen[:, 0, :], start=True, stop=False)
            T.matmul(bank[1][:, 2 * E:3 * E], ones[:], chosen[:, 1, :], start=False, stop=True).then_inc(pos_psum, 1)

            def gather(q, b):
                src, h = (h_hi, h_lo)[q // 2], q % 2
                for k in range(4):
                    kk = 4 * h + k
                    for i in range(NT):
                        last = T.matmul(bank[b][:, k * CAP:(k + 1) * CAP], src[:, i, kk * P:(kk + 1) * P],
                                        sel[:, i, :], start=(i == 0), stop=(i == NT - 1))
                last.then_inc(xe_psum, 1)

            pe.wait_ge(sel_ready, NT)
            pe.wait_ge(h_split, 4)
            gather(0, 1)
            gather(1, 3)
            gather(2, 7)
            pe.wait_ge(xe_hi_ready, 1)
            gather(3, 1)
            pe.wait_ge(trips_ready, 1)
            trips = pe.value_load(trips_i[0:1, 0:1], min_val=E, max_val=PASSES * E)
            with pe.Fori(0, trips) as j:
                def split_piece(kind, c, half, k):
                    t = BASE + xplace[kind, c, half]
                    pe.wait_ge(w_lo_ready, j * XS + (t + 1))
                    return split_views(t, k)

                def up(kind, c):
                    dst = bank[(0 if kind == "e1" else 2) + c % 2][:]
                    if kind == "e1" and c >= 2:
                        pe.wait_ge(act_ready, j * FCH + c - 1)
                    for half in range(2):
                        hi, lo = split_piece(kind, c, half, 4)
                        for k in range(4):
                            kk = 4 * half + k
                            T.matmul(dst, xe_hi[:, kk, :], hi[:, k, :], start=(kk == 0), stop=False)
                            T.matmul(dst, xe_hi[:, kk, :], lo[:, k, :], start=False, stop=False)
                            last = T.matmul(dst, xe_lo[:, kk, :], hi[:, k, :], start=False, stop=(kk == KD - 1))
                        last.then_inc(w_used, 1)

                def transposes(c):
                    pe.wait_ge(act_ready, j * FCH + c + 1)
                    if c >= 1:
                        pe.wait_ge(actT_ready, j * FCH + c)
                    for k in range(FB):
                        last = T.transpose(bank[4][:, k * P:(k + 1) * P], act[:, c % 2, k * P:(k + 1) * P], ident[:])
                    last.then_inc(actT_psum, 1)

                def down(c):
                    pe.wait_ge(actT_ready, j * FCH + c + 1)
                    for half in range(2):
                        hi, lo = split_piece("e2", c, half, 2)
                        for k in range(2):
                            f = slice((2 * half + k) * P, (2 * half + k + 1) * P)
                            first, end = c == 0 and half == 0 and k == 0, c == FCH - 1 and half == 1 and k == 1
                            for n in range(NH):
                                dst, r = bank[5 + n][:], slice(n * BANK, (n + 1) * BANK)
                                T.matmul(dst, actT_hi[:, f], hi[:, k, r], start=first, stop=False)
                                T.matmul(dst, actT_hi[:, f], lo[:, k, r], start=False, stop=False)
                                last = T.matmul(dst, actT_lo[:, f], hi[:, k, r], start=False, stop=end)
                        last.then_inc(w_used, 1)

                pe.wait_ge(xe_hi_ready, j * 2 + 2)
                pe.wait_ge(xe_lo_ready, j * 2 + 2)
                up("e1", 0)
                up("e3", 0)
                pe.wait_ge(added, j * 4 + 1)
                for c in range(1, FCH):
                    up("e1", c)
                    transposes(c - 1)
                    up("e3", c)
                    if c == FCH - 1:
                        pe.wait_ge(sel_ready, (j + 2) * NT)
                        pe.wait_ge(act_ready, j * FCH + FCH - 1)
                        pe.wait_ge(selT_ready, (j + 1) * 2)
                        gather(0, 1)
                        gather(1, 3)
                        gather(2, 7)
                    down(c - 1)
                    if c == 2:
                        pe.wait_ge(self_ready, (j + 1) * NT)
                        for i in range(NT):
                            T.transpose(bank[7][:, i * P:(i + 1) * P], sel_f[:, i, :], ident[:])
                        for i in range(NT):
                            last = T.matmul(bank[7][:, S:S + 1], sel_f[:, i, :], wgt_tab[:, i, bass.ds(j, 1)],
                                            start=(i == 0), stop=(i == NT - 1))
                        last.then_inc(selT_psum, 1)
                pe.wait_ge(xe_hi_ready, j * 2 + 3)
                gather(3, 1)
                transposes(FCH - 1)
                down(FCH - 1)
                pe.wait_ge(ye_lo_ready, (j + 1) * NH)
                pe.wait_ge(xe_hi_ready, j * 2 + 4)
                pe.wait_ge(xe_lo_ready, j * 2 + 4)
                for q, b in enumerate(BACK):
                    i, n = divmod(q, 2)
                    r, c = slice(i * P, (i + 1) * P), slice(n * BANK, (n + 1) * BANK)
                    T.matmul(bank[b][:], selT[:, r], ye_hi[:, c], start=True, stop=False)
                    T.matmul(bank[b][:], selT[:, r], ye_lo[:, c], start=False, stop=True).then_inc(back_psum, 1)


def kernel(**inputs):
    import numpy as np
    import concourse.bacc as bacc
    from concourse import mybir as mb
    from concourse.bass_utils import run_bass_kernel_spmd

    a = {name: np.asarray(v) for name, v in inputs.items()}
    B, S, D = a["x"].shape
    L, P = a["w_in"].shape[0], 128
    HD, KV, G = 64, 2, 4

    def cols(v):
        return v.reshape(L, -1, P).transpose(0, 2, 1)

    def both(v):
        return np.concatenate([v, v], axis=2).transpose(0, 2, 1)

    def positions(v):
        return v.reshape(L, -1, 2, HD).transpose(0, 2, 3, 1).reshape(L, P, -1)

    def second(v):
        return v.reshape(L, -1, P, HD).transpose(0, 2, 1, 3).reshape(L, P, -1)

    taps = a["conv_dw_w"].transpose(0, 2, 1)
    small = np.concatenate([
        cols(a["attn_norm_g"]), cols(a["ffn_norm_g"]),
        taps.reshape(L, -1, P, taps.shape[2]).transpose(0, 2, 1, 3).reshape(L, P, -1),
        cols(a["conv_dw_b"]), cols(a["conv_ln_g"]), cols(a["conv_ln_b"]),
        both(a["q_norm_g"][:, None, :]), both(a["k_norm_g"]),
        positions(a["cmp_pos_k"]), positions(a["cmp_pos_v"]),
        second(a["cmp_k_w2"]), second(a["cmp_v_w2"])], axis=2)
    rows = np.concatenate([a["cmp_k_b1"], a["cmp_v_b1"], a["cmp_k_b2"], a["cmp_v_b2"]], axis=1)
    wo = a["w_out"]
    half = wo.shape[1] // 2
    att = wo[:, half:].reshape(L, KV, G, HD, D).transpose(0, 2, 1, 3, 4).reshape(L, half, D)
    w_out = np.concatenate([wo[:, :half], att], axis=1)

    args = [("x", a["x"][0]), ("w_in", a["w_in"]), ("cmp_k_w1", a["cmp_k_w1"]), ("cmp_v_w1", a["cmp_v_w1"]),
            ("w_out", w_out), ("dense_w1", a["dense_w1"][0]), ("dense_w3", a["dense_w3"][0]),
            ("dense_w2", a["dense_w2"][0]), ("moe_w1", a["moe_w1"][0]), ("moe_w3", a["moe_w3"][0]),
            ("moe_w2", a["moe_w2"][0]), ("small", small), ("rows", rows), ("router", a["router_w"][0])]
    nc = bacc.Bacc("TRN2", target_bir_lowering=False, num_devices=1)
    arrays, aps = {}, []
    for name, v in args:
        v = np.ascontiguousarray(v)
        arrays["in_" + name] = v
        aps.append(nc.dram_tensor("in_" + name, v.shape, mb.dt.from_np(v.dtype), kind="ExternalInput").ap())
    out = nc.dram_tensor("out_0", (S, D), mb.dt.float32, kind="ExternalOutput").ap()
    hymba_trunk(nc, *aps, out)
    r = run_bass_kernel_spmd(nc, [arrays], core_ids=[0])
    return r.results[0]["out_0"].reshape(B, S, D)
```
